# Optimizing a Trainium2 kernel written in Bass

```python
import math
import jax
import jax.numpy as jnp
from jax import lax
import numpy as np

D_MODEL = 1024
BATCH = 1
SEQ = 256
DEPTH = 1
DEC_BATCH = 1
DEC_SEQ = 64
PAST_LEN = 128

CHUNK = 64
SSM_HEADS = 16
SSM_HEAD_DIM = 64
D_SSM = SSM_HEADS * SSM_HEAD_DIM
SSM_GROUPS = 2
D_STATE = 128
CONV_W = 4
D_CONV = D_SSM + 2 * SSM_GROUPS * D_STATE
SSD_CHUNK = CHUNK
ATT_HEADS = 8
ATT_HEAD_DIM = 64
D_ATT = ATT_HEADS * ATT_HEAD_DIM
LEFT_CHUNKS = 8
ATT_LEFT = LEFT_CHUNKS * CHUNK
BAND = ATT_LEFT + CHUNK
REL_CLIP = 128
ATT_SCALE = ATT_HEAD_DIM ** -0.5
D_MIX = D_SSM + D_ATT
D_IN_PROJ = D_SSM + D_CONV + SSM_HEADS + 3 * D_ATT
N_EXPERTS = 32
TOP_K = 4
D_FF = D_MODEL
SWIGLU_ALPHA = 1.702
SWIGLU_LIMIT = 7.0
MOE_BLOCK = 128
EPS = 1e-5

kernel_name = "hybrid_ssd_chunkattn_moe_stream_step"

def rms_norm(x, g):
    xf = x.astype(jnp.float32)
    y = xf * lax.rsqrt(jnp.mean(xf * xf, axis=-1, keepdims=True) + EPS)
    return (y * g.astype(jnp.float32)).astype(x.dtype)

def split_proj(h, w_in):
    u = h @ w_in
    cuts = [int(c) for c in np.cumsum([D_SSM, D_CONV, SSM_HEADS, D_ATT, D_ATT])]
    return jnp.split(u, cuts, axis=-1)

def causal_dwconv(u, prev, w, b):
    s = u.shape[1]
    up = jnp.concatenate([prev.astype(u.dtype), u], axis=1)
    y = b
    for tap in range(CONV_W):
        y = y + w[tap] * up[:, tap:tap + s]
    return y, up[:, -(CONV_W - 1):]

def ssd_scan(x, dt, a, bm, cm, h0):
    bsz, s = x.shape[:2]
    pad = (-s) % SSD_CHUNK
    if pad:
        padw = lambda t: jnp.pad(t, [(0, 0), (0, pad)] + [(0, 0)] * (t.ndim - 2))
        x, dt, bm, cm = padw(x), padw(dt), padw(bm), padw(cm)
    nc = (s + pad) // SSD_CHUNK
    L = SSD_CHUNK
    x = x.reshape(bsz, nc, L, SSM_HEADS, SSM_HEAD_DIM)
    dt = dt.reshape(bsz, nc, L, SSM_HEADS)
    bm = bm.reshape(bsz, nc, L, SSM_HEADS, D_STATE)
    cm = cm.reshape(bsz, nc, L, SSM_HEADS, D_STATE)
    a_cum = jnp.cumsum(dt * a, axis=2)
    xdt = x * dt[..., None]
    seg = a_cum[:, :, :, None, :] - a_cum[:, :, None, :, :]
    causal = jnp.tril(jnp.ones((L, L), dtype=bool))[None, None, :, :, None]
    decay = jnp.exp(jnp.where(causal, seg, -jnp.inf))
    scores = jnp.einsum('bclhn,bcshn->bclsh', cm, bm) * decay
    y_diag = jnp.einsum('bclsh,bcshp->bclhp', scores, xdt)
    decay_to_end = jnp.exp(a_cum[:, :, -1:, :] - a_cum)
    chunk_states = jnp.einsum('bclhn,bclhp->bchpn', bm * decay_to_end[..., None], xdt)
    chunk_decay = jnp.exp(a_cum[:, :, -1, :])

    def step(h_prev, inp):
        st, dc = inp
        return h_prev * dc[:, :, None, None] + st, h_prev

    h_final, h_enter = lax.scan(step, h0, (jnp.swapaxes(chunk_states, 0, 1), jnp.swapaxes(chunk_decay, 0, 1)))
    h_enter = jnp.swapaxes(h_enter, 0, 1)
    y_off = jnp.einsum('bclhn,bchpn->bclhp', cm, h_enter) * jnp.exp(a_cum)[..., None]
    y = (y_diag + y_off).reshape(bsz, nc * L, SSM_HEADS, SSM_HEAD_DIM)[:, :s]
    return y, h_final

def ssd_mixer(z, xbc, dt_raw, conv_prev, h0, conv_w, conv_b, dt_bias, a_log, d_skip, norm_g):
    bsz, s = z.shape[:2]
    xbc, conv_state = causal_dwconv(xbc, conv_prev, conv_w, conv_b)
    xbc = jax.nn.silu(xbc).astype(jnp.float32)
    xs, bm, cm = jnp.split(xbc, [D_SSM, D_SSM + SSM_GROUPS * D_STATE], axis=-1)
    xs = xs.reshape(bsz, s, SSM_HEADS, SSM_HEAD_DIM)
    rep = SSM_HEADS // SSM_GROUPS
    bm = jnp.repeat(bm.reshape(bsz, s, SSM_GROUPS, D_STATE), rep, axis=2)
    cm = jnp.repeat(cm.reshape(bsz, s, SSM_GROUPS, D_STATE), rep, axis=2)
    dt = jax.nn.softplus(dt_raw.astype(jnp.float32) + dt_bias.astype(jnp.float32))
    a = -jnp.exp(a_log.astype(jnp.float32))
    y, h_final = ssd_scan(xs, dt, a, bm, cm, h0.astype(jnp.float32))
    y = y + d_skip.astype(jnp.float32)[:, None] * xs
    y = y.reshape(bsz, s, D_SSM).astype(z.dtype) * jax.nn.silu(z)
    y = rms_norm(y.reshape(bsz, s, SSM_GROUPS, D_SSM // SSM_GROUPS), norm_g.reshape(SSM_GROUPS, -1))
    return y.reshape(bsz, s, D_SSM), conv_state, h_final

def rel_bias(table, rel):
    return table[:, jnp.clip(rel, -REL_CLIP, REL_CLIP) + REL_CLIP]

def band_attention_prompt(q, k, v, table):
    bsz, s = q.shape[:2]
    nc = s // CHUNK
    qc = q.reshape(bsz, nc, CHUNK, ATT_HEADS, ATT_HEAD_DIM)
    padc = ((0, 0), (LEFT_CHUNKS, 0), (0, 0), (0, 0), (0, 0))
    kc = jnp.pad(k.reshape(bsz, nc, CHUNK, ATT_HEADS, ATT_HEAD_DIM), padc)
    vc = jnp.pad(v.reshape(bsz, nc, CHUNK, ATT_HEADS, ATT_HEAD_DIM), padc)
    kb = jnp.stack([kc[:, j:j + nc] for j in range(LEFT_CHUNKS + 1)], axis=2).reshape(bsz, nc, BAND, ATT_HEADS, ATT_HEAD_DIM)
    vb = jnp.stack([vc[:, j:j + nc] for j in range(LEFT_CHUNKS + 1)], axis=2).reshape(bsz, nc, BAND, ATT_HEADS, ATT_HEAD_DIM)
    qi = jnp.arange(CHUNK)
    kj = jnp.arange(BAND)
    bias = rel_bias(table, ATT_LEFT + qi[:, None] - kj[None, :])
    key_pos = jnp.arange(nc)[:, None] * CHUNK - ATT_LEFT + kj[None, :]
    valid = (key_pos >= 0)[None, :, None, None, :]
    scores = jnp.einsum('bcqhd,bckhd->bchqk', qc, kb).astype(jnp.float32) * ATT_SCALE
    scores = jnp.where(valid, scores + bias[None, None].astype(jnp.float32), -jnp.inf)
    p = jax.nn.softmax(scores, axis=-1)
    o = jnp.einsum('bchqk,bckhd->bcqhd', p.astype(v.dtype), vb)
    return o.reshape(bsz, s, ATT_HEADS, ATT_HEAD_DIM)

def band_attention_step(q, k_new, v_new, k_cache, v_cache, table):
    t = q.shape[1]
    w = k_cache.shape[1]
    keys = jnp.concatenate([k_cache.astype(k_new.dtype), k_new], axis=1)
    vals = jnp.concatenate([v_cache.astype(v_new.dtype), v_new], axis=1)
    rel = (w + jnp.arange(t))[:, None] - jnp.arange(w + t)[None, :]
    scores = jnp.einsum('bqhd,bkhd->bhqk', q, keys).astype(jnp.float32) * ATT_SCALE
    scores = scores + rel_bias(table, rel)[None].astype(jnp.float32)
    p = jax.nn.softmax(scores, axis=-1)
    return jnp.einsum('bhqk,bkhd->bqhd', p.astype(vals.dtype), vals)

def merge_heads(y_ssm, o_att, att_norm_g, w_out):
    o = rms_norm(o_att.reshape(o_att.shape[0], o_att.shape[1], D_ATT), att_norm_g)
    return jnp.concatenate([y_ssm, o], axis=-1) @ w_out

def moe_ffn(h, w_router, b_router, w_gate_up, b_gate_up, w_down, b_down):
    xt = h.reshape(-1, D_MODEL)
    n_tok = xt.shape[0]
    logits = (xt @ w_router + b_router).astype(jnp.float32)
    top_val, top_idx = lax.top_k(logits, TOP_K)
    gates = jax.nn.softmax(top_val, axis=-1)
    n_assign = n_tok * TOP_K
    flat_e = top_idx.reshape(-1)
    order = jnp.argsort(flat_e)
    sorted_e = flat_e[order]
    sorted_tok = order // TOP_K
    sorted_gate = gates.reshape(-1)[order]
    counts = jnp.bincount(flat_e, length=N_EXPERTS)
    padded = (counts + MOE_BLOCK - 1) // MOE_BLOCK * MOE_BLOCK
    pad_end = jnp.cumsum(padded)
    pad_start = pad_end - padded
    start = jnp.cumsum(counts) - counts
    dest = pad_start[sorted_e] + jnp.arange(n_assign) - start[sorted_e]
    n_blocks = -(-n_assign // MOE_BLOCK) + N_EXPERTS
    rows = n_blocks * MOE_BLOCK
    row_tok = jnp.full((rows,), n_tok, jnp.int32).at[dest].set(sorted_tok.astype(jnp.int32))
    x_rows = jnp.concatenate([xt, jnp.zeros((1, D_MODEL), xt.dtype)], axis=0)[row_tok]
    x_rows = x_rows.reshape(n_blocks, MOE_BLOCK, D_MODEL)
    block_expert = jnp.minimum(jnp.searchsorted(pad_end, jnp.arange(n_blocks) * MOE_BLOCK, side='right'), N_EXPERTS - 1)

    def expert_block(args):
        xb, e = args
        gu = xb @ w_gate_up[e] + b_gate_up[e]
        gate = jnp.minimum(gu[:, :D_FF], SWIGLU_LIMIT)
        up = jnp.clip(gu[:, D_FF:], -SWIGLU_LIMIT, SWIGLU_LIMIT)
        act = (up + 1) * gate * jax.nn.sigmoid(gate * SWIGLU_ALPHA)
        return act @ w_down[e] + b_down[e]

    y_rows = lax.map(expert_block, (x_rows, block_expert)).reshape(rows, D_MODEL)
    contrib = y_rows[dest] * sorted_gate[:, None].astype(y_rows.dtype)
    out = jnp.zeros_like(xt).at[sorted_tok].add(contrib)
    return out.reshape(h.shape)

def setup_inputs(seed: int = 0) -> dict:
    key = jax.random.key(seed)
    ks = jax.random.split(key, 25)
    f32 = jnp.float32
    nrm = lambda k, shape, s: jax.random.normal(k, shape, f32) * s
    att_rows = min(ATT_LEFT, PAST_LEN)
    dt0 = jnp.exp(jax.random.uniform(ks[10], (DEPTH, SSM_HEADS), f32, math.log(1e-3), math.log(1e-1)))
    return {
        'x_prompt': nrm(ks[0], (BATCH, SEQ, D_MODEL), 1.0),
        'x_sample': nrm(ks[1], (DEC_BATCH, DEC_SEQ, D_MODEL), 1.0),
        'cache_k': nrm(ks[2], (DEPTH, DEC_BATCH, att_rows, ATT_HEADS, ATT_HEAD_DIM), 1.0),
        'cache_v': nrm(ks[3], (DEPTH, DEC_BATCH, att_rows, ATT_HEADS, ATT_HEAD_DIM), 1.0),
        'state_conv': nrm(ks[4], (DEPTH, DEC_BATCH, CONV_W - 1, D_CONV), 1.0),
        'state_ssm': nrm(ks[5], (DEPTH, DEC_BATCH, SSM_HEADS, SSM_HEAD_DIM, D_STATE), 0.1),
        'norm_mix_g': 1.0 + nrm(ks[6], (DEPTH, D_MODEL), 0.02),
        'w_in': nrm(ks[7], (DEPTH, D_MODEL, D_IN_PROJ), D_MODEL ** -0.5),
        'conv_w': nrm(ks[8], (DEPTH, CONV_W, D_CONV), CONV_W ** -0.5),
        'conv_b': nrm(ks[9], (DEPTH, D_CONV), 0.02),
        'dt_bias': dt0 + jnp.log(-jnp.expm1(-dt0)),
        'a_log': jnp.log(jax.random.uniform(ks[11], (DEPTH, SSM_HEADS), f32, 1.0, 16.0)),
        'd_skip': 1.0 + nrm(ks[12], (DEPTH, SSM_HEADS), 0.1),
        'ssm_norm_g': 1.0 + nrm(ks[13], (DEPTH, D_SSM), 0.02),
        'att_norm_g': 1.0 + nrm(ks[14], (DEPTH, D_ATT), 0.02),
        'rel_bias_table': nrm(ks[15], (DEPTH, ATT_HEADS, 2 * REL_CLIP + 1), 0.1),
        'w_out': nrm(ks[16], (DEPTH, D_MIX, D_MODEL), D_MIX ** -0.5),
        'norm_ffn_g': 1.0 + nrm(ks[17], (DEPTH, D_MODEL), 0.02),
        'w_router': nrm(ks[18], (DEPTH, D_MODEL, N_EXPERTS), D_MODEL ** -0.5),
        'b_router': nrm(ks[19], (DEPTH, N_EXPERTS), 0.01),
        'w_gate_up': nrm(ks[20], (DEPTH, N_EXPERTS, D_MODEL, 2 * D_FF), D_MODEL ** -0.5),
        'b_gate_up': nrm(ks[21], (DEPTH, N_EXPERTS, 2 * D_FF), 0.02),
        'w_down': nrm(ks[22], (DEPTH, N_EXPERTS, D_FF, D_MODEL), D_FF ** -0.5),
        'b_down': nrm(ks[23], (DEPTH, N_EXPERTS, D_MODEL), 0.02),
        'norm_final_g': 1.0 + nrm(ks[24], (D_MODEL,), 0.02),
    }

def reference(x_prompt, x_sample, cache_k, cache_v, state_conv, state_ssm,
              norm_mix_g, w_in, conv_w, conv_b, dt_bias, a_log, d_skip, ssm_norm_g,
              att_norm_g, rel_bias_table, w_out, norm_ffn_g, w_router, b_router,
              w_gate_up, b_gate_up, w_down, b_down, norm_final_g):
    xp, xs = x_prompt, x_sample
    bp, sp = x_prompt.shape[:2]
    bd, sd = x_sample.shape[:2]
    keep = min(ATT_LEFT, sp)
    k_p, v_p, conv_p, ssm_p = [], [], [], []
    k_s, v_s, conv_s, ssm_s = [], [], [], []
    for l in range(DEPTH):
        hp = rms_norm(xp, norm_mix_g[l])
        z, xbc, dtr, q, k, v = split_proj(hp, w_in[l])
        conv0 = jnp.zeros((bp, CONV_W - 1, D_CONV), xp.dtype)
        h0 = jnp.zeros((bp, SSM_HEADS, SSM_HEAD_DIM, D_STATE), jnp.float32)
        y_ssm, cst, hst = ssd_mixer(z, xbc, dtr, conv0, h0, conv_w[l], conv_b[l], dt_bias[l],
                                    a_log[l], d_skip[l], ssm_norm_g[l])
        q, k, v = [t.reshape(bp, sp, ATT_HEADS, ATT_HEAD_DIM) for t in (q, k, v)]
        o = band_attention_prompt(q, k, v, rel_bias_table[l])
        xp = xp + merge_heads(y_ssm, o, att_norm_g[l], w_out[l])
        xp = xp + moe_ffn(rms_norm(xp, norm_ffn_g[l]), w_router[l], b_router[l],
                          w_gate_up[l], b_gate_up[l], w_down[l], b_down[l])
        k_p.append(k[:, sp - keep:])
        v_p.append(v[:, sp - keep:])
        conv_p.append(cst)
        ssm_p.append(hst.astype(state_ssm.dtype))
        hs = rms_norm(xs, norm_mix_g[l])
        z, xbc, dtr, q, k, v = split_proj(hs, w_in[l])
        y_ssm, cst, hst = ssd_mixer(z, xbc, dtr, state_conv[l], state_ssm[l], conv_w[l], conv_b[l],
                                    dt_bias[l], a_log[l], d_skip[l], ssm_norm_g[l])
        q, k, v = [t.reshape(bd, sd, ATT_HEADS, ATT_HEAD_DIM) for t in (q, k, v)]
        o = band_attention_step(q, k, v, cache_k[l], cache_v[l], rel_bias_table[l])
        xs = xs + merge_heads(y_ssm, o, att_norm_g[l], w_out[l])
        xs = xs + moe_ffn(rms_norm(xs, norm_ffn_g[l]), w_router[l], b_router[l],
                          w_gate_up[l], b_gate_up[l], w_down[l], b_down[l])
        k_s.append(k)
        v_s.append(v)
        conv_s.append(cst)
        ssm_s.append(hst.astype(state_ssm.dtype))
    y_prompt = rms_norm(xp, norm_final_g)
    y_sample = rms_norm(xs, norm_final_g)
    return (y_prompt, y_sample,
            jnp.stack(k_p), jnp.stack(v_p), jnp.stack(conv_p), jnp.stack(ssm_p),
            jnp.stack(k_s), jnp.stack(v_s), jnp.stack(conv_s), jnp.stack(ssm_s))


_drawn_inputs = setup_inputs


def setup_inputs(seed=0):
    import zlib

    import numpy as np

    out = dict(_drawn_inputs(seed))
    spreads = {}
    factors = {'b_gate_up': 6.84, 'b_down': 7.736, 'norm_final_g': 2.837}
    for name, (base, spread) in spreads.items():
        noise = np.random.default_rng([zlib.crc32(name.encode()), seed]).standard_normal(out[name].shape)
        drawn = base * np.exp(spread * noise) if base else spread * noise
        out[name] = jnp.asarray(drawn.astype(out[name].dtype))
    for name, factor in factors.items():
        out[name] = (out[name] * factor).astype(out[name].dtype)
    return out
```

```python
import numpy as np
import concourse.bass as bass
from concourse import mybir
from contextlib import ExitStack

D = 1024
SP, SS = 256, 64
HEADS, P_HEAD, NSTATE, GROUPS = 16, 64, 128, 2
D_SSM = HEADS * P_HEAD
D_CONV = D_SSM + 2 * GROUPS * NSTATE
TAPS = 4
AH, AD = 8, 64
D_ATT = AH * AD
D_MIX = D_SSM + D_ATT
PAST = 128
CLIP = 128
NREL = 2 * CLIP + 1
NE, TOPK, F = 32, 4, 1024
EPS = 1e-5
ALPHA, LIMIT = 1.702, 7.0
NEG = -1.0e30

ROWS = [128, 128, 64]
NT = 3
HCOL = [0, 128, 259]
HC = 323
TCOL = [0, 128, 256]
TC = 320
KD = D // 128
CT = D_CONV // 128
XT = D_SSM // 128
MT = D_MIX // 128
SLOTS, SLOT = 6, 4096
CAP = 64
HALF = 512

C_Z, C_XBC, C_DT = 0, D_SSM, D_SSM + D_CONV
C_Q = C_DT + HEADS
W_IN_CHUNKS = [C_XBC, C_XBC + 512, C_XBC + 1024, C_Q, C_Q + 512, C_Q + 1024, C_Z, C_Z + 512]
N_IN, N_OUT = len(W_IN_CHUNKS), 3
FRONT = N_IN + N_OUT
GU_CHUNKS, DN_CHUNKS = 4, 2
N_SMALL = 21
MAX_BLOCKS = NE + TC * TOPK // CAP


def build(nc, x_prompt, x_sample, cache_k, cache_v, state_conv, state_ssm,
          norm_mix_g, w_in, conv_w, conv_b, dt_bias, a_log, d_skip, ssm_norm_g,
          att_norm_g, rel_bias_table, w_out, norm_ffn_g, w_router, b_router,
          w_gate_up, b_gate_up, w_down, b_down, norm_final_g,
          y_prompt, y_sample, k_prompt, v_prompt, conv_prompt, ssm_prompt,
          k_sample, v_sample, conv_sample, ssm_sample):
    f32, i32, u32, f32r = mybir.dt.float32, mybir.dt.int32, mybir.dt.uint32, mybir.dt.float32r
    ALU = mybir.AluOpType
    ACT = mybir.ActivationFunctionType
    X = mybir.AxisListType.X
    ctx = ExitStack()
    with ctx:
        def sb(name, shape, dt=f32):
            return ctx.enter_context(nc.sbuf_tensor(name, shape, dt))

        def sem(name):
            return ctx.enter_context(nc.semaphore(name))

        ring = sb("ring", [128, SLOTS, SLOT])
        r1 = sb("r1", [128, 3072])
        r2 = sb("r2", [128, 2584])
        r3 = sb("r3", [128, 3912])
        r4 = sb("r4", [128, 3876])
        r5 = sb("r5", [128, 2584])
        r6 = sb("r6", [128, 4096])
        with ExitStack() as early:
            def sb_early(name, shape):
                return early.enter_context(nc.sbuf_tensor(name, shape, f32))

            vt = sb_early("vt", [128, NT, D_ATT])
            ot = sb_early("ot", [128, NT, D_ATT])
            ck = sb_early("ck", [128, D_ATT])
            cv = sb_early("cv", [128, D_ATT])
            ckT = sb_early("ckT", [128, 4, PAST])
        b_gu2 = sb("b_gu2", [128, 2, HALF], f32r)
        b_dn2 = sb("b_dn2", [128, 2, HALF], f32r)
        yy2 = sb("yy2", [128, 2, HALF], f32r)
        c01 = sb("c01", [128, 2, TC], f32r)
        sel = sb("sel", [128, 4, CAP], f32r)
        sel_dn = sb("sel_dn", [128, 2, CAP], f32r)
        lg = sb("lg", [128, NT, NE])
        one = sb("one", [128, NT, NE])
        gate = sb("gate", [128, NT, NE])
        chosen = sb("chosen", [128, NT, NE])
        pg = sb("pg", [128, NE, 2 * NT])
        pcur = sb("pcur", [128, 2 * NT])
        gprev = sb("gprev", [128, NT])
        nbk = sb("nbk", [128, 4, NE])
        bej = sb("bej", [128, 2])
        before = sb("before", [1, NE], i32)
        blocks = sb("blocks", [1, 1], i32)
        expert_of = sb("expert_of", [1, 128], i32)
        place_of = sb("place_of", [1, 128], i32)

        def view(region, at, *dims):
            n = int(np.prod(dims))
            v = region[:, at:at + n]
            if len(dims) == 2:
                return v.rearrange("p (a b) -> p a b", b=dims[1])
            if len(dims) == 3:
                return v.rearrange("p (a b c) -> p a b c", b=dims[1], c=dims[2])
            return v

        x = view(r1, 0, NT, D)
        z = view(r1, 0, NT, D)
        hT = view(r2, 0, KD, HC)
        kt = view(r2, 0, NT, D_ATT)
        s_out = view(r2, 1536, 8, NSTATE)
        pad = view(r3, 0, CT, HC + 3)
        xs = view(r3, 0, NT, D)
        bt = view(r3, 3072, NT, 256)
        xn = view(r3, 0, NT, D)
        praw = r4[0:88, 0:128]
        lgT = r4[0:NE, 0:TC]
        conv = view(r4, 0, CT, HC)
        mixT = view(r4, 0, MT, TC)
        qk = view(r5, 0, 8, HC)
        hst = view(r5, 0, D_SSM)
        s_raw = view(r5, 1024, 8, NSTATE)
        hraw = view(r6, 0, D_CONV)
        tab = r6[0:AH, 1536:1536 + NREL]
        ext = r6[0:AH, 1800:2183]
        iota_i = r6[:, 2200:2200 + TC].bitcast(i32)
        pidx_i = r6[:, 2199:2200].bitcast(i32)
        dtT = r6[0:HEADS, 2624:2624 + HC]
        bias = view(r6, 0, AH, 256)
        sc = view(r6, 2048, 4, 256)
        pT = view(r6, 3072, 8, 128)
        cso = view(r6, 2048, D_CONV)
        scratch = view(r6, 3072, D)
        dau = view(r6, 0, 8, 128)
        ee = view(r6, 1024, 8, 128)
        xdt = view(r6, 2048, 8, P_HEAD)
        xw = view(r6, 2560, 8, P_HEAD)
        yo = view(r6, 3072, 8, P_HEAD)
        gm = view(r6, 3584, GROUPS, 128)
        hfT = view(r6, 0, KD, TC)
        xe = view(r6, 0, HALF)
        xt = view(r6, 512, 4, 2, CAP)
        ug = view(r6, 1024, HALF)
        sg = view(r6, 1536, HALF)
        uu = view(r6, 2048, HALF)
        ac = view(r6, 2560, HALF)
        at = view(r6, 3072, 4, 2, CAP)
        pm = view(r2, 0, NT, 128)
        gfin = view(r2, 1536, D)

        b_gu = sb("b_gu", [128, HALF])
        b_dn = sb("b_dn", [128, HALF])
        ident = sb("ident", [128, 128])
        upper = sb("upper", [128, 128])
        strict = sb("strict", [128, 128])
        lower = sb("lower", [128, 128])
        ones = sb("ones", [128, 128])
        iota = sb("iota", [128, TC])
        prevT = sb("prevT", [128, CT, 3])
        cst = sb("cst", [128, CT, 6])
        par = sb("par", [128, 88])
        gmix, gffn, gout, cb = par[:, 0:8], par[:, 8:16], par[:, 16:28], par[:, 28:40]
        cw = par[:, 40:88].rearrange("p (j c) -> p c j", j=TAPS)
        wdt = sb("wdt", [128, KD, HEADS])
        wr = sb("wr", [128, KD, NE])
        brt = sb("brt", [NE, 1])
        dtb = sb("dtb", [128, HEADS])
        alog = sb("alog", [128, HEADS])
        dsk = sb("dsk", [128, HEADS])
        dta = sb("dta", [128, NT, HEADS])
        dtt = sb("dtt", [128, NT, HEADS])
        dt = sb("dt", [128, NT, HEADS])
        dA = sb("dA", [128, NT, HEADS])
        edec = sb("edec", [128, NT, 48])
        stat = sb("stat", [128, 12])
        mx = sb("mx", [128, 4])
        sm = sb("sm", [128, 4])
        rs = sb("rs", [128, 4])
        m8 = sb("m8", [128, NT, 8])
        i8 = sb("i8", [128, NT, 8], u32)
        ix = sb("ix", [128, NT, 8])
        pv = sb("pv", [128, NT, 4])
        ps4 = sb("ps4", [128, NT])
        pidx = sb("pidx", [128, 1])
        PS = ctx.enter_context(nc.psum_tensor("PS", [128, 8, 512], f32))
        table_d = nc.dram_tensor("bias_table_clipped", (AH, 383), f32)

        names = """consts par_mm par_ready x_in small_in state_in cache_in bcast_in biasrow_in cvhist_in ext_out bias_in sraw_in
            xres_in gfin_in
            ssq rstd xnorm hT_mm hT_ready hist_mm ck_mm ck_ready proj_mm proj_ev w_used w_dt
            conv_done silu_done prev_ready t2_mm t2_dve t2_act dtc_ready expdt ln_done dA_ready
            cst_ready cst_mm cso_ready cso_out ktv_out
            qk_mm sc_ready mx_ready exp_ready pT_mm pT_ready pv_mm o_ready
            dau_ready cum_mm seg_mm seg_exp gt_mm gm_ready ed_ready m_ready xw_ready y_mm y_ev
            hst_mm hst_ev sraw_mm sraw_ev sout_out
            ssq2 sqrt2 mixn mixT_mm mixT_ready out_mm x1_ready ssq3 sqrt3 xn_ready
            hf_mm hf_ready lg_mm lgT_ready lgt_mm rexp pv_ready pos_mm route_ready
            p_ready xe_mm ct_mm xe_ev xt_mm xt_ev gu_mm gs_used gs_used1 gs_used2 ds_used
            g_ready gu_ev sig_ready act_ready comb_mm o_ev c_ready at_mm at_ev d_mm yy_ready
            before_ready bej_ready bej_mm b2_ready b_hi yyl_ready sel_ready seld_ready pcur_ready gates_held
            ssq4 sqrt4 fin_ready y_out vchain achain pchain""".split()
        s = {n: sem(n) for n in names}
        w_full = [sem(f"w_full{i}") for i in range(SLOTS)]
        block = ctx.enter_context(nc.Block())

        def bank(b, rows=128):
            return PS[0:rows, b, :]

        def bc(ap, *shape):
            return ap.to_broadcast(list(shape))

        def slot_of(chunk):
            return chunk % SLOTS

        @block.sync
        def _(sp):
            def load(chunk, dst, src):
                sp.dma_start(dst, src).then_inc(w_full[slot_of(chunk)], 16)

            def wait_used(i):
                if i < N_IN:
                    sp.wait_ge(s["proj_mm"], 4 * i + 4 if i < 5 else 21 + 3 * (i - 4))
                else:
                    sp.wait_ge(s["out_mm"], 6)

            for t in range(2):
                sp.dma_start(x[:, t, :], x_prompt[0, 128 * t:128 * t + 128, :]).then_inc(s["x_in"], 16)
            sp.dma_start(x[0:SS, 2, :], x_sample[0, :, :]).then_inc(s["x_in"], 16)
            sp.wait_ge(s["x_in"], 48)
            sp.wait_ge(s["small_in"], N_SMALL * 16)
            w3 = w_in[0].rearrange("(k p) n -> p k n", p=128)
            for i, c in enumerate(W_IN_CHUNKS):
                if i >= SLOTS:
                    wait_used(i - SLOTS)
                load(i, ring[:, slot_of(i), :].rearrange("p (k n) -> p k n", k=KD), w3[:, :, c:c + 512])
            wo = w_out[0].rearrange("(k p) n -> p k n", p=128)
            for j in range(N_OUT):
                i = N_IN + j
                wait_used(i - SLOTS)
                load(i, ring[:, slot_of(i), :].rearrange("p (k n) -> p k n", k=4), wo[:, 4 * j:4 * j + 4, :])

            gu = w_gate_up[0]
            dn = w_down[0]

            def load_gu(e, c, first):
                src = gu[bass.ds(e, 1)].rearrange("a (k p) n -> p (a k) n", p=128)[:, 2 * c:2 * c + 2, :]
                load(first, ring[:, slot_of(first), :].rearrange("p (k n) -> p k n", k=2), src)

            def load_dn(e, c, first):
                src = dn[bass.ds(e, 1)].rearrange("a (k p) n -> p (a k) n", p=128)[:, 4 * c:4 * c + 4, :]
                load(first, ring[:, slot_of(first), :].rearrange("p (k n) -> p k n", k=4), src)

            for c in range(GU_CHUNKS + DN_CHUNKS):
                wait_used(FRONT + c - SLOTS)
                if c < GU_CHUNKS:
                    load_gu(0, c, FRONT + c)
                else:
                    load_dn(0, c - GU_CHUNKS, FRONT + c)
            sp.wait_ge(s["route_ready"], 1)
            used = ["gs_used", "gs_used1", "gs_used2", "gu_mm", "ds_used", "d_mm"]
            with sp.Fori(1, NE) as e:
                first = sp.value_load(before[0:1, bass.ds(e, 1)], min_val=1, max_val=MAX_BLOCKS)
                for c in range(GU_CHUNKS + DN_CHUNKS):
                    sp.wait_ge(s[used[c]], first)
                    if c < GU_CHUNKS:
                        load_gu(e, c, FRONT + c)
                    else:
                        load_dn(e, c - GU_CHUNKS, FRONT + c)
            for t in range(2):
                sp.wait_ge(s["fin_ready"], t + 1)
                sp.dma_start(y_prompt[0, 128 * t:128 * t + 128, :], xn[:, t, :]).then_inc(s["y_out"], 16)
            sp.wait_ge(s["fin_ready"], 3)
            sp.dma_start(y_sample[0, :, :], xn[0:SS, 2, :]).then_inc(s["y_out"], 16)
            sp.wait_ge(s["y_out"], 48)
            sp.wait_ge(s["ktv_out"], 6 * 16)
            sp.wait_ge(s["cso_out"], 2 * 16)
            sp.wait_ge(s["sout_out"], 2 * 16)

        @block.gpsimd
        def _(pool):
            g = nc.gpsimd
            npc = [0]

            def step(ins):
                npc[0] += 1
                ins.then_inc(s["pchain"], 1)
                pool.wait_ge(s["pchain"], npc[0])

            for m in (upper, strict, lower, ident, ones):
                step(g.memset(m[:, :], 0.0 if m is ident else 1.0))
            step(g.affine_select(out=ident[:, :], in_=ident[:, :], compare_op=ALU.not_equal, fill=1.0,
                                 base=0, pattern=[[-1, 128]], channel_multiplier=1))
            step(g.affine_select(out=upper[:, :], in_=upper[:, :], compare_op=ALU.is_ge, fill=0.0,
                                 base=0, pattern=[[1, 128]], channel_multiplier=-1))
            step(g.affine_select(out=strict[:, :], in_=strict[:, :], compare_op=ALU.is_gt, fill=0.0,
                                 base=0, pattern=[[1, 128]], channel_multiplier=-1))
            step(g.affine_select(out=lower[:, :], in_=lower[:, :], compare_op=ALU.is_gt, fill=0.0,
                                 base=0, pattern=[[-1, 128]], channel_multiplier=1))
            step(g.iota(iota_i, pattern=[[1, TC]], base=0, channel_multiplier=0))
            step(g.tensor_copy(iota[:, :], iota_i))
            step(g.iota(pidx_i, pattern=[[0, 1]], base=0, channel_multiplier=1))
            step(g.tensor_copy(pidx[:, :], pidx_i))
            step(g.memset(b_dn[64:128, :], 0.0))
            step(g.memset(pad[:, :, 0:3], 0.0))
            step(g.memset(hT[:, :, 256:259], 0.0))
            g.memset(stat[:, :], 1.0).then_inc(s["consts"], 1)

            pool.wait_ge(s["ck_ready"], 1)
            for t in range(NT):
                rows = ROWS[t]
                kd = k_prompt[0, 0, 128 * t:128 * t + 128] if t < 2 else k_sample[0, 0]
                vd = v_prompt[0, 0, 128 * t:128 * t + 128] if t < 2 else v_sample[0, 0]
                pool.wait_ge(s["t2_act"], t + 1)
                pool.dma_start(kd.rearrange("n h d -> n (h d)"), kt[0:rows, t, :]).then_inc(s["ktv_out"], 16)
                pool.dma_start(vd.rearrange("n h d -> n (h d)"), vt[0:rows, t, :]).then_inc(s["ktv_out"], 16)
            pool.wait_ge(s["cso_ready"], 3)
            pool.dma_start(conv_prompt[0, 0], cso[0:3, :]).then_inc(s["cso_out"], 16)
            pool.dma_start(conv_sample[0, 0], cso[3:6, :]).then_inc(s["cso_out"], 16)
            pool.wait_ge(s["qk_mm"], 6)
            pool.dma_start(s_raw, state_ssm[0, 0].rearrange("(c a) p n -> (a p) c n", a=2)).then_inc(s["sraw_in"], 16)
            for n, dst in enumerate((ssm_prompt, ssm_sample)):
                pool.wait_ge(s["hst_ev"], 2 * n + 2)
                pool.dma_start(dst[0, 0].rearrange("(c a) p n -> (a p) c n", a=2), s_out).then_inc(s["sout_out"], 16)
            pool.wait_ge(s["mixT_mm"], 9)
            for t in range(2):
                pool.dma_start(x[:, t, :], x_prompt[0, 128 * t:128 * t + 128, :]).then_inc(s["xres_in"], 16)
            pool.dma_start(x[0:SS, 2, :], x_sample[0, :, :]).then_inc(s["xres_in"], 16)
            pool.wait_ge(s["ktv_out"], 6 * 16)
            pool.wait_ge(s["sout_out"], 2 * 16)
            pool.dma_start(gfin, norm_final_g.rearrange("(a n) -> a n", a=1).to_broadcast([128, D])).then_inc(s["gfin_in"], 16)

        @block.scalar
        def _(act):
            a = nc.scalar
            ac_n = [0]

            def step(ins):
                ac_n[0] += 1
                ins.then_inc(s["achain"], 1)
                act.wait_ge(s["achain"], ac_n[0])

            def small(dst, src):
                act.dma_start(dst, src).then_inc(s["small_in"], 16)

            for at0, src in ((0, norm_mix_g[0]), (8, norm_ffn_g[0]), (16, ssm_norm_g[0]), (24, att_norm_g[0]), (28, conv_b[0])):
                k = src.shape[0] // 128
                small(praw[at0:at0 + k, :], src.rearrange("(k p) -> k p", p=128))
            small(praw[40:88, :], conv_w[0].rearrange("j (k p) -> (j k) p", p=128))
            small(brt[:, :], b_router[0].rearrange("(e a) -> e a", a=1))
            small(dtb[:, :], dt_bias[0:1, :].to_broadcast([128, HEADS]))
            small(alog[:, :], a_log[0:1, :].to_broadcast([128, HEADS]))
            small(dsk[:, :], d_skip[0:1, :].to_broadcast([128, HEADS]))
            small(tab[:, :], rel_bias_table[0])
            small(wr[:, :, :], w_router[0].rearrange("(k p) n -> p k n", p=128))
            small(wdt[:, :, :], w_in[0].rearrange("(k p) n -> p k n", p=128)[:, :, C_DT:C_DT + HEADS])
            small(ck[:, :], cache_k[0, 0].rearrange("n h d -> n (h d)"))
            small(cv[:, :], cache_v[0, 0].rearrange("n h d -> n (h d)"))
            for c in range(4):
                small(b_gu[32 * c:32 * c + 32, :], b_gate_up[0][:, 512 * c:512 * c + 512])
            for c in range(2):
                small(b_dn[32 * c:32 * c + 32, :], b_down[0][:, 512 * c:512 * c + 512])
            act.dma_start(hraw[0:3], state_conv[0, 0]).then_inc(s["cvhist_in"], 16)
            act.wait_ge(s["consts"], 1)
            act.wait_ge(s["x_in"], 48)
            for t in range(NT):
                step(a.activation(scratch[0:ROWS[t]], x[0:ROWS[t], t, :], ACT.Square,
                                  accum_out=stat[0:ROWS[t], t:t + 1]))
            a.activation(stat[:, 3:6], stat[:, 0:3], ACT.Copy).then_inc(s["ssq"], 1)
            act.wait_ge(s["rstd"], 1)
            a.activation(stat[:, 0:3], stat[:, 3:6], ACT.Sqrt).then_inc(s["ssq"], 1)
            act.wait_ge(s["ext_out"], 1)
            act.dma_start(table_d.ap(), ext[:, :]).then_inc(s["ext_out"], 16)
            act.wait_ge(s["ext_out"], 17)
            act.wait_ge(s["hist_mm"], 1)
            for q in range(4):
                act.dma_start(bias[:, 2 * q:2 * q + 2, :], bass.AP(
                    table_d, head_of(q // 2, 2 * (q % 2)) * 383, [[1, 128], [2 * 383, 2], [1, 256]]))\
                    .then_inc(s["bias_in"], 16)

            def out_of(n, dst, src, func=ACT.Copy):
                act.wait_ge(s["proj_mm"], n + 1)
                a.activation(dst, src, func).then_inc(s["proj_ev"], 1)

            n = 0
            for c in range(CT):
                out_of(n, pad[:, c, 3:3 + HC], PS[:, n % 4, 0:HC])
                n += 1
            for c in range(8):
                out_of(n, qk[:, c, :], PS[:, n % 4, 0:HC])
                n += 1
            out_of(n, dtT[:, :], PS[0:HEADS, n % 4, 0:HC])
            n += 1
            for t in range(NT):
                out_of(n, vt[0:ROWS[t], t, :], PS[0:ROWS[t], n % 4, :])
                n += 1
            for c in range(3):
                act.wait_ge(s["conv_done"], 4 * c + 4)
                a.activation(conv[:, 4 * c:4 * c + 4, :], conv[:, 4 * c:4 * c + 4, :], ACT.Silu)\
                    .then_inc(s["silu_done"], 1)
            for h in range(2):
                for t in range(NT):
                    out_of(n, z[0:ROWS[t], t, 512 * h:512 * h + 512], PS[0:ROWS[t], n % 4, :], ACT.Silu)
                    n += 1
            act.wait_ge(s["dtc_ready"], 1)
            step(a.activation(alog[:, :], alog[:, :], ACT.Exp))
            step(a.activation(dtt[:, :, :], dta[:, :, :], ACT.Exp, scale=-1.0))
            a.activation(dtt[:, :, :], dtt[:, :, :], ACT.Ln, bias=1.0).then_inc(s["ln_done"], 1)
            for t in range(NT):
                act.wait_ge(s["t2_mm"], 3 * t + 4)
                a.activation(kt[0:ROWS[t], t, :], PS[0:ROWS[t], 7, :], ACT.Copy).then_inc(s["t2_act"], 1)
            for i in range(6):
                t, rows = i // 2, ROWS[i // 2]
                nk = (128, 256, PAST + SS)[t]
                act.wait_ge(s["mx_ready"], i + 1)
                for h in range(4):
                    last = a.activation(sc[0:rows, h, 0:nk], sc[0:rows, h, 0:nk], ACT.Exp,
                                        bias=mx[0:rows, h:h + 1], accum_out=sm[0:rows, h:h + 1])
                last.then_inc(s["exp_ready"], 1)
            for i in range(6):
                t, rows = i // 2, ROWS[i // 2]
                if i % 2 == 0:
                    act.wait_ge(s["cum_mm"], t + 1)
                    a.activation(edec[0:rows, t, 0:32], PS[0:rows, 0, 0:32], ACT.Exp)
                    a.activation(edec[:, t, 32:48], PS[:, 0, 32:48], ACT.Exp).then_inc(s["ed_ready"], 1)
                act.wait_ge(s["seg_mm"], i + 1)
                if i:
                    act.wait_ge(s["y_mm"], i)
                a.activation(ee[0:rows, :, 0:rows], seg_ps(PS, rows), ACT.Exp).then_inc(s["seg_exp"], 1)
            act.wait_ge(s["y_ev"], 6)
            act.wait_ge(s["o_ready"], 6)
            for t in range(NT):
                rows = ROWS[t]
                for gg in range(GROUPS):
                    step(a.activation(dau_flat(r6, rows), z[0:rows, t, 512 * gg:512 * gg + 512], ACT.Square,
                                      accum_out=stat[0:rows, 2 * t + gg:2 * t + gg + 1]))
                step(a.activation(dau_flat(r6, rows), ot[0:rows, t, :], ACT.Square,
                                  accum_out=stat[0:rows, 6 + t:7 + t]))
            a.activation(stat[:, 11:12], stat[:, 8:9], ACT.Copy).then_inc(s["ssq2"], 1)
            act.wait_ge(s["ssq2"], 2)
            a.activation(stat[:, 0:9], stat[:, 0:9], ACT.Sqrt).then_inc(s["sqrt2"], 1)
            for t in range(NT):
                act.wait_ge(s["x1_ready"], 2 * t + 2)
                step(a.activation(r6[0:ROWS[t], 3072:4096], x[0:ROWS[t], t, :], ACT.Square,
                                  accum_out=stat[0:ROWS[t], t:t + 1]))
                a.activation(stat[0:ROWS[t], 3 + t:4 + t], stat[0:ROWS[t], t:t + 1], ACT.Sqrt,
                             scale=1.0 / D, bias=stat[0:ROWS[t], 10:11]).then_inc(s["sqrt3"], 1)
            act.wait_ge(s["rexp"], 1)
            a.activation(pv[:, :, :], pv[:, :, :], ACT.Exp).then_inc(s["pv_ready"], 1)

            act.wait_ge(s["mixT_mm"], 9)
            step(a.activation(b_gu2[:, 0, :], b_gu[:, :], ACT.Copy))
            a.activation(b_dn2[:, 0, :], b_dn[:, :], ACT.Copy).then_inc(s["b_hi"], 1)

            act.wait_ge(s["route_ready"], 1)
            for free in ("c_ready", "at_ev", "yy_ready"):
                act.sem_inc(s[free], 1)
            total = act.value_load(blocks[0:1, 0:1], min_val=NE, max_val=MAX_BLOCKS)
            act.wait_ge(s["xe_mm"], 1)
            a.activation(xe, bank(3), ACT.Copy).then_inc(s["xe_ev"], 1)
            with act.Fori(0, total) as b:
                act.wait_ge(s["ct_mm"], b + 1)
                act.wait_ge(s["comb_mm"], 6 * b + 6)
                a.activation(c01[0:64, 0, :], PS[0:64, 5, 0:TC], ACT.Copy)
                a.activation(c01[64:128, 1, :], PS[64:128, 5, 0:TC], ACT.Copy).then_inc(s["c_ready"], 1)
                act.wait_ge(s["g_ready"], b + 1)
                a.activation(sg, ug, ACT.Sigmoid, scale=ALPHA).then_inc(s["sig_ready"], 1)
                act.wait_ge(s["xe_mm"], b + 2)
                a.activation(xe, bank(3), ACT.Copy).then_inc(s["xe_ev"], 1)
                act.wait_ge(s["at_mm"], b + 1)
                a.activation(at.rearrange("p a b c -> p (a b c)"), bank(4), ACT.Copy).then_inc(s["at_ev"], 1)
                act.wait_ge(s["d_mm"], b + 1)
                a.activation(yy2[:, 0, :], bank(2), ACT.Copy).then_inc(s["yy_ready"], 1)
            for t in range(NT):
                act.wait_ge(s["o_ev"], 6 * total + 2 * t + 4)
                step(a.activation(r6[0:ROWS[t], 0:D], x[0:ROWS[t], t, :], ACT.Square,
                                  accum_out=stat[0:ROWS[t], t:t + 1]))
                a.activation(stat[0:ROWS[t], 3 + t:4 + t], stat[0:ROWS[t], t:t + 1], ACT.Sqrt,
                             scale=1.0 / D, bias=stat[0:ROWS[t], 10:11]).then_inc(s["sqrt4"], 1)

        @block.vector
        def _(dve):
            v = nc.vector
            vc = [0]

            def step(ins):
                vc[0] += 1
                ins.then_inc(s["vchain"], 1)
                dve.wait_ge(s["vchain"], vc[0])

            dve.wait_ge(s["small_in"], N_SMALL * 16)
            dve.wait_ge(s["consts"], 1)
            v.tensor_copy(ext[:, 0:256], tab[:, 1:NREL])
            v.tensor_copy(ext[:, 256:383], bc(tab[:, 2 * CLIP:NREL], AH, 127)).then_inc(s["ext_out"], 1)
            dve.wait_ge(s["par_mm"], 1)
            v.tensor_copy(par[:, :], PS[:, 7, 0:88]).then_inc(s["par_ready"], 1)
            dve.wait_ge(s["ssq"], 1)
            v.tensor_scalar(stat[:, 3:6], stat[:, 3:6], 1.0 / D, EPS, ALU.mult, ALU.add).then_inc(s["rstd"], 1)
            dve.wait_ge(s["ssq"], 2)
            step(v.reciprocal(stat[:, 3:6], stat[:, 0:3]))
            for t in range(NT):
                rows = ROWS[t]
                v.tensor_scalar(x[0:rows, t, :], x[0:rows, t, :], stat[0:rows, 3 + t:4 + t], None, ALU.mult)\
                    .then_inc(s["xnorm"], 1)
            for i in range(6):
                t, h, rows = i // 2, i % 2, ROWS[i // 2]
                dve.wait_ge(s["hT_mm"], i + 1)
                v.tensor_tensor(hT[:, 4 * h:4 * h + 4, HCOL[t]:HCOL[t] + rows],
                                PS[:, i, :].rearrange("p (k n) -> p k n", k=4)[:, :, 0:rows],
                                bc(gmix[:, 4 * h:4 * h + 4].unsqueeze(2), 128, 4, rows), ALU.mult)\
                    .then_inc(s["hT_ready"], 1)
            dve.wait_ge(s["ck_mm"], 1)
            v.tensor_copy(ckT[:, :, :], bank(7).rearrange("p (k n) -> p k n", k=4)).then_inc(s["ck_ready"], 1)
            dve.wait_ge(s["hist_mm"], 1)
            step(v.tensor_copy(prevT[:, :, :], PS[:, 6, 0:36].rearrange("p (k n) -> p k n", n=3)))
            for c in range(CT):
                dve.wait_ge(s["proj_ev"], c + 1)
                step(v.tensor_copy(pad[:, c, 259:262], prevT[:, c, :]))
                step(v.tensor_scalar(conv[:, c, :], pad[:, c, 0:HC], cw[:, c, 0:1], cb[:, c:c + 1], ALU.mult, ALU.add))
                for j in range(1, TAPS):
                    ins = v.scalar_tensor_tensor(conv[:, c, :], pad[:, c, j:j + HC], cw[:, c, j:j + 1],
                                                 conv[:, c, :], ALU.mult, ALU.add)
                    if j < TAPS - 1:
                        step(ins)
                ins.then_inc(s["conv_done"], 1)
            v.tensor_copy(cst[:, :, 0:3], pad[:, :, 256:259])
            v.tensor_copy(cst[:, :, 3:6], pad[:, :, HC:HC + 3]).then_inc(s["cst_ready"], 1)
            dve.wait_ge(s["cst_ready"], 1)
            dve.wait_ge(s["t2_mm"], 1)
            step(v.memset(dta[:, 2, :], 0.0))
            for t in range(NT):
                step(v.tensor_tensor(dA[0:ROWS[t], t, :], PS[0:ROWS[t], 4, 16 * t:16 * t + 16],
                                     dtb[0:ROWS[t], :], ALU.add))
            step(v.memset(dA[64:128, 2, :], 0.0))
            step(v.tensor_scalar(dt[:, :, :], dA[:, :, :], -1.0, None, ALU.mult))
            v.tensor_tensor(dta[:, :, :], dA[:, :, :], dt[:, :, :], ALU.max).then_inc(s["dtc_ready"], 1)
            for t in range(NT):
                rows = ROWS[t]
                dve.wait_ge(s["t2_mm"], 3 * t + 2)
                v.tensor_copy(xs[0:rows, t, 0:512], PS[0:rows, 5, :]).then_inc(s["t2_dve"], 1)
                dve.wait_ge(s["t2_mm"], 3 * t + 3)
                v.tensor_copy(xs[0:rows, t, 512:1024], PS[0:rows, 6, :]).then_inc(s["t2_dve"], 1)
                dve.wait_ge(s["t2_mm"], 3 * t + 4)
                v.tensor_copy(bt[0:rows, t, :], PS[0:rows, 4, 64:320]).then_inc(s["t2_dve"], 1)
            for i in range(3):
                dve.wait_ge(s["cst_mm"], i + 1)
                v.tensor_copy(cso[0:6, 512 * i:512 * i + 512], PS[0:6, i, :]).then_inc(s["cso_ready"], 1)
            dve.wait_ge(s["ln_done"], 1)
            step(v.tensor_scalar(dA[:, :, :], dA[:, :, :], 0.0, None, ALU.max))
            step(v.tensor_tensor(dt[:, :, :], dA[:, :, :], dtt[:, :, :], ALU.add))
            step(v.scalar_tensor_tensor(dA[:, :, :], dt[:, :, :], -1.0,
                                        bc(alog[:, :].unsqueeze(1), 128, NT, HEADS), ALU.mult, ALU.mult))
            dve.wait_ge(s["bias_in"], 64)
            step(v.memset(bias[0:64, :, 0:64], NEG))
            dve.wait_ge(s["cso_out"], 32)
            for i in range(7):
                if i < 6:
                    t, hg, rows = i // 2, i % 2, ROWS[i // 2]
                    nk, b0 = ((128, 128), (256, 0), (PAST + SS, 0))[t]
                    dve.wait_ge(s["qk_mm"], i + 1)
                    if i:
                        dve.wait_ge(s["pT_mm"], i)
                    step(v.scalar_tensor_tensor(
                        sc[0:rows, :, 0:nk],
                        PS[0:rows, 2 * (i % 2):2 * (i % 2) + 2, :].rearrange("p b (h n) -> p (b h) n", h=2)[:, :, 0:nk],
                        float(AD) ** -0.5, backwards(bias[0:rows, 4 * hg:4 * hg + 4, :], 255 - b0, nk), ALU.mult, ALU.add))
                    if i:
                        if i > 1:
                            dve.wait_ge(s["o_ready"], i - 1)
                        step(v.reciprocal(rs[:, :], sm[:, :]))
                    v.tensor_reduce(mx[0:rows, :], sc[0:rows, :, 0:nk], axis=X, op=ALU.max, negate=True)\
                        .then_inc(s["mx_ready"], 1)
                if i:
                    tp, hp, rp = (i - 1) // 2, (i - 1) % 2, ROWS[(i - 1) // 2]
                    if i == 6:
                        dve.wait_ge(s["o_ready"], i - 1)
                        step(v.reciprocal(rs[:, :], sm[:, :]))
                    dve.wait_ge(s["pv_mm"], i)
                    v.tensor_tensor(ot[0:rp, tp, 256 * hp:256 * hp + 256].rearrange("p (h b d) -> p b h d", b=2, d=AD),
                                    PS[0:rp, 6, 0:256].rearrange("p (b h d) -> p b h d", b=2, d=AD),
                                    bc(rs[0:rp, :].rearrange("p (b h) -> p b h", b=2).unsqueeze(3), rp, 2, 2, AD),
                                    ALU.mult).then_inc(s["o_ready"], 1)
                if i < 6:
                    nt = 8 if nk > 128 else 4
                    dve.wait_ge(s["pT_mm"], i + 1)
                    v.tensor_copy(pT[:, 0:nt, 0:rows],
                                  PS[:, 4:6, :].rearrange("p b (h n) -> p (b h) n", h=4)[:, 0:nt, 0:rows])\
                        .then_inc(s["pT_ready"], 1)
            for i in range(6):
                t, gg, rows = i // 2, i % 2, ROWS[i // 2]
                hs = slice(8 * gg, 8 * gg + 8)
                if i == 0:
                    dve.wait_ge(s["o_ready"], 6)
                v.tensor_tensor(dau[0:rows, :, 0:rows], bc(dA[0:rows, t, hs].unsqueeze(2), rows, 8, rows),
                                bc(upper[0:rows, 0:rows].unsqueeze(1), rows, 8, rows), ALU.mult)\
                    .then_inc(s["dau_ready"], 1)
                if gg == 0:
                    dve.wait_ge(s["gt_mm"], t + 1)
                    step(v.tensor_tensor(gm[0:rows, :, 0:rows],
                                         PS[0:rows, 1, 0:256].rearrange("p (g n) -> p g n", g=2)[:, :, 0:rows],
                                         bc(upper[0:rows, 0:rows].unsqueeze(1), rows, 2, rows), ALU.mult))
                    dve.wait_ge(s["ed_ready"], t + 1)
                xh = xs[0:rows, t, 512 * gg:512 * gg + 512].rearrange("p (h d) -> p h d", d=P_HEAD)
                if i:
                    dve.wait_ge(s["y_ev"], i)
                step(v.tensor_tensor(xdt[0:rows], xh, bc(dt[0:rows, t, hs].unsqueeze(2), rows, 8, P_HEAD), ALU.mult))
                v.tensor_tensor(xw[0:rows], xdt[0:rows],
                                bc(edec[0:rows, t, 16 + 8 * gg:24 + 8 * gg].unsqueeze(2), rows, 8, P_HEAD), ALU.mult)\
                    .then_inc(s["xw_ready"], 1)
                dve.wait_ge(s["seg_exp"], i + 1)
                v.tensor_tensor(ee[0:rows, :, 0:rows], ee[0:rows, :, 0:rows],
                                bc(gm[0:rows, gg, 0:rows].unsqueeze(1), rows, 8, rows), ALU.mult)\
                    .then_inc(s["m_ready"], 1)
                dve.wait_ge(s["y_mm"], i + 1)
                zh = z[0:rows, t, 512 * gg:512 * gg + 512].rearrange("p (h d) -> p h d", d=P_HEAD)
                heads = lambda b, r: PS[0:r, b, :].rearrange("p (h d) -> p h d", d=P_HEAD)
                hh = hst[:, 512 * gg:512 * gg + 512].rearrange("p (h d) -> p h d", d=P_HEAD)
                step(v.tensor_tensor(xdt[0:rows], xh, bc(dsk[0:rows, hs].unsqueeze(2), rows, 8, P_HEAD), ALU.mult))
                step(v.tensor_tensor(xdt[0:rows], xdt[0:rows], heads(4, rows), ALU.add))
                if t:
                    step(v.tensor_tensor(yo[0:rows], heads(5, rows),
                                         bc(edec[0:rows, t, 8 * gg:8 * gg + 8].unsqueeze(2), rows, 8, P_HEAD), ALU.mult))
                    step(v.tensor_tensor(xdt[0:rows], xdt[0:rows], yo[0:rows], ALU.add))
                    step(v.tensor_tensor(hh, hh, bc(edec[:, t, 32 + 8 * gg:40 + 8 * gg].unsqueeze(2), 128, 8, P_HEAD), ALU.mult))
                    step(v.tensor_tensor(hh, hh, heads(6, 128), ALU.add))
                else:
                    step(v.tensor_copy(hh, heads(6, 128)))
                v.tensor_tensor(zh, xdt[0:rows], zh, ALU.mult).then_inc(s["y_ev"], 1)
                if i in (3, 5):
                    for q in range(2):
                        n = 2 * (i // 4) + q
                        dve.wait_ge(s["hst_mm"], n + 1)
                        if i == 5 and q == 0:
                            dve.wait_ge(s["sout_out"], 16)
                        v.tensor_copy(s_out[:, 4 * q:4 * q + 4, :], PS[:, (7, 1)[q], :].rearrange("p (k n) -> p k n", k=4))\
                            .then_inc(s["hst_ev"], 1)
                if i == 3:
                    for q in range(2):
                        dve.wait_ge(s["sraw_mm"], q + 1)
                        v.tensor_copy(hst[:, 512 * q:512 * q + 512], bank((7, 1)[q])).then_inc(s["sraw_ev"], 1)
            dve.wait_ge(s["ssq2"], 1)
            v.tensor_scalar(stat[:, 0:9], stat[:, 0:9], 1.0 / 512, EPS, ALU.mult, ALU.add).then_inc(s["ssq2"], 1)
            dve.wait_ge(s["sqrt2"], 1)
            step(v.reciprocal(stat[:, 0:9], stat[:, 0:9]))
            for t in range(NT):
                rows = ROWS[t]
                for gg in range(GROUPS):
                    zz = z[0:rows, t, 512 * gg:512 * gg + 512]
                    v.tensor_scalar(zz, zz, stat[0:rows, 2 * t + gg:2 * t + gg + 1], None, ALU.mult)\
                        .then_inc(s["mixn"], 1)
                v.tensor_scalar(ot[0:rows, t, :], ot[0:rows, t, :], stat[0:rows, 6 + t:7 + t], None, ALU.mult)\
                    .then_inc(s["mixn"], 1)
            for i in range(9):
                t, q, rows = i // 3, i % 3, ROWS[i // 3]
                dve.wait_ge(s["mixT_mm"], i + 1)
                v.tensor_tensor(mixT[:, 4 * q:4 * q + 4, TCOL[t]:TCOL[t] + rows],
                                PS[:, i % 4, :].rearrange("p (k n) -> p k n", k=4)[:, :, 0:rows],
                                bc(gout[:, 4 * q:4 * q + 4].unsqueeze(2), 128, 4, rows), ALU.mult)\
                    .then_inc(s["mixT_ready"], 1)
            step(v.memset(stat[:, 10:11], EPS))
            step(v.memset(xn[:, 2, :], 0.0))
            dve.wait_ge(s["xres_in"], 48)
            for t in range(NT):
                rows = ROWS[t]
                for h in range(2):
                    i = 2 * t + h
                    dve.wait_ge(s["out_mm"], i + 1)
                    xx = x[0:rows, t, 512 * h:512 * h + 512]
                    v.tensor_tensor(xx, xx, PS[0:rows, 4 + i % 4, :], ALU.add).then_inc(s["x1_ready"], 1)
            for t in range(NT):
                rows = ROWS[t]
                dve.wait_ge(s["sqrt3"], t + 1)
                step(v.reciprocal(stat[0:rows, 6 + t:7 + t], stat[0:rows, 3 + t:4 + t]))
                v.tensor_scalar(xn[0:rows, t, :], x[0:rows, t, :], stat[0:rows, 6 + t:7 + t], None, ALU.mult)\
                    .then_inc(s["xn_ready"], 1)
                for h in range(2):
                    i = 2 * t + h
                    dve.wait_ge(s["hf_mm"], i + 1)
                    v.tensor_tensor(hfT[:, 4 * h:4 * h + 4, TCOL[t]:TCOL[t] + rows],
                                    PS[:, i % 4, :].rearrange("p (k n) -> p k n", k=4)[:, :, 0:rows],
                                    bc(gffn[:, 4 * h:4 * h + 4].unsqueeze(2), 128, 4, rows), ALU.mult)\
                        .then_inc(s["hf_ready"], 1)
            dve.wait_ge(s["lg_mm"], 1)
            v.tensor_scalar(lgT[:, :], PS[0:NE, 4, 0:TC], brt[:, 0:1], None, ALU.add).then_inc(s["lgT_ready"], 1)
            step(v.memset(lg[:, :, :], 0.0))
            step(v.memset(pg[:, :, :], -1.0))
            dve.wait_ge(s["lgt_mm"], 1)
            for t in range(NT):
                step(v.tensor_copy(lg[0:ROWS[t], t, :], PS[0:ROWS[t], 5, 32 * t:32 * t + 32]))
            for t in range(NT):
                step(v.max(m8[:, t, :], lg[:, t, :]))
                step(v.max_index(i8[:, t, :], m8[:, t, :], lg[:, t, :]))
            step(v.tensor_copy(ix[:, :, :], i8[:, :, :]))
            v.tensor_tensor(pv[:, :, :], m8[:, :, 0:4], bc(m8[:, :, 0:1], 128, NT, 4), ALU.subtract)\
                .then_inc(s["rexp"], 1)
            dve.wait_ge(s["pv_ready"], 1)
            step(v.tensor_reduce(ps4[:, :], pv[:, :, :], axis=X, op=ALU.add))
            step(v.reciprocal(ps4[:, :], ps4[:, :]))
            step(v.tensor_tensor(pv[:, :, :], pv[:, :, :], bc(ps4[:, :].unsqueeze(2), 128, NT, 4), ALU.mult))
            for t in range(NT):
                step(v.tensor_scalar(gate[:, t, :], iota[:, 0:NE], ix[:, t, 0:1], pv[:, t, 0:1], ALU.is_equal, ALU.mult))
                for k in range(1, TOPK):
                    step(v.tensor_scalar(one[:, t, :], iota[:, 0:NE], ix[:, t, k:k + 1], pv[:, t, k:k + 1],
                                         ALU.is_equal, ALU.mult))
                    step(v.tensor_tensor(gate[:, t, :], gate[:, t, :], one[:, t, :], ALU.add))
            v.tensor_scalar(chosen[:, :, :], gate[:, :, :], 0.0, None, ALU.is_gt).then_inc(s["rexp"], 1)
            dve.wait_ge(s["pos_mm"], 1)
            for t in range(NT):
                rows = ROWS[t]
                step(v.scalar_tensor_tensor(one[0:rows, t, :], PS[0:rows, 6, 32 * t:32 * t + 32], 1.0,
                                            chosen[0:rows, t, :], ALU.add, ALU.mult))
                step(v.tensor_scalar(pg[0:rows, :, t], one[0:rows, t, :], -1.0, None, ALU.add))
                step(v.tensor_copy(pg[0:rows, :, NT + t], gate[0:rows, t, :]))
            count, nb, upto, t3 = PS[:, 6, 96:128], nbk[:, 0, :], nbk[:, 1, :], nbk[:, 2, :]
            step(v.memset(nbk[:, 3, :], 0.0))
            step(v.tensor_scalar(nb, count, float(CAP), 1.0, ALU.is_gt, ALU.add))
            for m in range(2, TC // CAP):
                step(v.scalar_tensor_tensor(nb, count, float(CAP * m), nb, ALU.is_gt, ALU.add))
            step(v.tensor_tensor_scan(upto, nb, nbk[:, 3, :], 0.0, ALU.add, ALU.add))
            step(v.tensor_scalar(t3, upto, pidx[:, 0:1], None, ALU.is_le))
            step(v.tensor_reduce(bej[:, 0:1], t3, axis=X, op=ALU.add))
            step(v.tensor_tensor(t3, t3, nb, ALU.mult))
            step(v.tensor_reduce(bej[:, 1:2], t3, axis=X, op=ALU.add))
            step(v.tensor_scalar(bej[:, 0:1], bej[:, 0:1], float(NE - 1), None, ALU.min))
            v.tensor_tensor(bej[:, 1:2], pidx[:, :], bej[:, 1:2], ALU.subtract).then_inc(s["bej_ready"], 1)
            step(v.tensor_tensor(t3[0:1], upto[0:1], nb[0:1], ALU.subtract))
            step(v.tensor_copy(before[:, :], t3[0:1]))
            step(v.tensor_copy(blocks[:, :], upto[0:1, NE - 1:NE]))
            dve.wait_ge(s["b_hi"], 1)
            step(v.tensor_tensor(b_gu2[:, 1, :], b_gu[:, :], b_gu2[:, 0, :].bitcast(f32), ALU.subtract))
            step(v.tensor_tensor(b_dn2[:, 1, :], b_dn[:, :], b_dn2[:, 0, :].bitcast(f32), ALU.subtract))
            step(v.memset(c01[:, :, :].bitcast(f32), 0.0))
            step(v.memset(gprev[:, :], 0.0))
            step(v.memset(yy2[:, :, :].bitcast(f32), 0.0))
            dve.wait_ge(s["bej_mm"], 1)
            step(v.tensor_copy(expert_of[:, :], PS[0:1, 7, 0:128]))
            v.tensor_scalar(place_of[:, :], PS[0:1, 7, 128:256], 0.0, None, ALU.max).then_inc(s["route_ready"], 1)
            dve.wait_ge(s["route_ready"], 1)
            dve.sem_inc(s["o_ev"], 2)
            for free in ("gu_ev", "yyl_ready", "gates_held"):
                dve.sem_inc(s[free], 1)
            total = dve.value_load(blocks[0:1, 0:1], min_val=NE, max_val=MAX_BLOCKS)

            def one_hots(b, e, j):
                v.tensor_copy(pcur[:, :], pg[:, bass.ds(e, 1), :].rearrange("p a n -> p (a n)")).then_inc(s["pcur_ready"], 1)
                dve.wait_ge(s["pcur_ready"], b + 1)
                for t in range(NT):
                    v.tensor_scalar(pm[:, t, :].rearrange("p (a n) -> p a n", a=2),
                                    bc(iota[:, bass.ds(j * CAP, CAP)].unsqueeze(1), 128, 2, CAP),
                                    pcur[:, t:t + 1], None, ALU.is_equal).then_inc(s["p_ready"], 1)

            def selector(dst, e, n, name):
                v.tensor_copy(dst, bc(ident[:, 0:NE * n].rearrange("p (c e) -> p c e", e=NE)[:, :, bass.ds(e, 1)],
                                      128, n, CAP)).then_inc(s[name], 1)

            def gathered(b):
                dve.wait_ge(s["xt_mm"], b + 1)
                v.tensor_tensor(xt, bank(3).rearrange("p (c h n) -> p c h n", c=4, h=2),
                                bc(gffn[:, :].rearrange("p (h c) -> p c h", h=2).unsqueeze(3), 128, 4, 2, CAP),
                                ALU.mult).then_inc(s["xt_ev"], 1)

            def accumulate(n):
                for i in range(6):
                    t, h, rows = i // 2, i % 2, ROWS[i // 2]
                    dve.wait_ge(s["comb_mm"], n + i + 1)
                    xx = x[0:rows, t, 512 * h:512 * h + 512]
                    v.scalar_tensor_tensor(xx, PS[0:rows, 6 + h, :], gprev[0:rows, t:t + 1], xx, ALU.mult, ALU.add)\
                        .then_inc(s["o_ev"], 1)

            one_hots(0, 0, 0)
            selector(sel[:, :, :], 0, 4, "sel_ready")
            gathered(0)
            with dve.Fori(0, total) as b:
                e = dve.value_load(expert_of[0:1, bass.ds(b, 1)], min_val=0, max_val=NE - 1)
                e_next = dve.value_load(expert_of[0:1, bass.ds(b + 1, 1)], min_val=0, max_val=NE - 1)
                j_next = dve.value_load(place_of[0:1, bass.ds(b + 1, 1)], min_val=0, max_val=TC // CAP - 1)
                selector(sel_dn[:, :, :], e, 2, "seld_ready")
                dve.wait_ge(s["gates_held"], b + 1)
                accumulate(6 * b)
                dve.wait_ge(s["o_ev"], 6 * b + 8)
                v.tensor_copy(gprev[:, :], pcur[:, NT:2 * NT]).then_inc(s["gates_held"], 1)
                dve.wait_ge(s["gates_held"], b + 2)
                dve.wait_ge(s["ct_mm"], b + 1)
                one_hots(b + 1, e_next, j_next)
                dve.wait_ge(s["gs_used"], b + 1)
                selector(sel[:, :, :], e_next, 4, "sel_ready")
                dve.wait_ge(s["gu_mm"], b + 1)
                v.tensor_scalar(ug, bank(0), LIMIT, None, ALU.min).then_inc(s["g_ready"], 1)
                v.tensor_scalar(uu, bank(1), LIMIT, -LIMIT, ALU.min, ALU.max).then_inc(s["gu_ev"], 1)
                dve.wait_ge(s["sig_ready"], b + 1)
                v.tensor_tensor(ug, ug, sg, ALU.mult).then_inc(s["act_ready"], 1)
                dve.wait_ge(s["act_ready"], 2 * b + 1)
                v.scalar_tensor_tensor(ac, uu, 1.0, ug, ALU.add, ALU.mult).then_inc(s["act_ready"], 1)
                gathered(b + 1)
                dve.wait_ge(s["yy_ready"], b + 2)
                v.tensor_tensor(yy2[:, 1, :], bank(2), yy2[:, 0, :].bitcast(f32), ALU.subtract)\
                    .then_inc(s["yyl_ready"], 1)
            dve.wait_ge(s["gates_held"], total + 1)
            accumulate(6 * total)
            dve.wait_ge(s["gfin_in"], 16)
            for t in range(NT):
                rows = ROWS[t]
                dve.wait_ge(s["sqrt4"], t + 1)
                step(v.reciprocal(stat[0:rows, 6 + t:7 + t], stat[0:rows, 3 + t:4 + t]))
                v.scalar_tensor_tensor(xn[0:rows, t, :], x[0:rows, t, :], stat[0:rows, 6 + t:7 + t],
                                       gfin[0:rows], ALU.mult, ALU.mult).then_inc(s["fin_ready"], 1)

        @block.tensor
        def _(pe):
            mm = nc.tensor.matmul

            def tr(out, in_):
                k = in_.shape[0]
                return nc.tensor.transpose(out, in_, ident[0:k, 0:k])

            pe.wait_ge(s["consts"], 1)
            pe.wait_ge(s["small_in"], N_SMALL * 16)
            tr(PS[:, 7, 0:88], praw[:, :]).then_inc(s["par_mm"], 1)
            for i in range(6):
                t, h, rows = i // 2, i % 2, ROWS[i // 2]
                pe.wait_ge(s["xnorm"], t + 1)
                for q in range(4):
                    k = 4 * h + q
                    last = tr(PS[:, i, 128 * q:128 * q + rows], x[0:rows, t, 128 * k:128 * k + 128])
                last.then_inc(s["hT_mm"], 1)
            pe.wait_ge(s["par_ready"], 1)
            for q in range(4):
                last = tr(PS[:, 7, 128 * q:128 * q + 128], ck[:, 128 * q:128 * q + 128])
            last.then_inc(s["ck_mm"], 1)
            pe.wait_ge(s["cvhist_in"], 16)
            for c in range(CT):
                last = tr(PS[:, 6, 3 * c:3 * c + 3], hraw[0:3, 128 * c:128 * c + 128])
            last.then_inc(s["hist_mm"], 1)
            pe.wait_ge(s["hT_ready"], 6)
            n = [0]

            def group(emit):
                if n[0] >= 4:
                    pe.wait_ge(s["proj_ev"], n[0] - 3)
                last = emit(n[0] % 4)
                last.then_inc(s["proj_mm"], 1)
                n[0] += 1

            def chunk(i):
                pe.wait_ge(w_full[slot_of(i)], 16 * (i // SLOTS + 1))
                return ring[:, slot_of(i), :].rearrange("p (k n) -> p k n", k=KD)

            def features(w, m):
                def emit(b):
                    for k in range(KD):
                        last = mm(PS[:, b, 0:HC], w[:, k, 128 * m:128 * m + 128], hT[:, k, :],
                                  start=(k == 0), stop=(k == KD - 1))
                    return last
                return emit

            def tokens(w, t):
                def emit(b):
                    for k in range(KD):
                        last = mm(PS[0:ROWS[t], b, :], hT[:, k, HCOL[t]:HCOL[t] + ROWS[t]], w[:, k, :],
                                  start=(k == 0), stop=(k == KD - 1))
                    return last
                return emit

            def dt_rows(b):
                for k in range(KD):
                    last = mm(PS[0:HEADS, b, 0:HC], wdt[:, k, :], hT[:, k, :], start=(k == 0), stop=(k == KD - 1))
                return last

            for i in range(5):
                w = chunk(i)
                for m in range(4):
                    group(features(w, m))
            group(dt_rows)
            for i in range(5, 8):
                w = chunk(i)
                for t in range(NT):
                    group(tokens(w, t))
            for t in range(NT):
                last = tr(PS[0:ROWS[t], 4, 16 * t:16 * t + 16], dtT[:, HCOL[t]:HCOL[t] + ROWS[t]])
            last.then_inc(s["t2_mm"], 1)
            pe.wait_ge(s["silu_done"], 3)
            pe.wait_ge(s["dtc_ready"], 1)
            for t in range(NT):
                rows, hc = ROWS[t], slice(HCOL[t], HCOL[t] + ROWS[t])
                for h in range(2):
                    if t:
                        pe.wait_ge(s["t2_dve"], 3 * t - 2 + h)
                    for q in range(4):
                        last = tr(PS[0:rows, 5 + h, 128 * q:128 * q + 128], conv[:, 4 * h + q, hc])
                    last.then_inc(s["t2_mm"], 1)
                if t:
                    pe.wait_ge(s["t2_dve"], 3 * t)
                    pe.wait_ge(s["t2_act"], t)
                for q in range(2):
                    tr(PS[0:rows, 4, 64 + 128 * q:64 + 128 * q + 128], conv[:, XT + q, hc])
                for q in range(4):
                    last = tr(PS[0:rows, 7, 128 * q:128 * q + 128], qk[:, 4 + q, hc])
                last.then_inc(s["t2_mm"], 1)
            pe.wait_ge(s["cst_ready"], 1)
            pe.wait_ge(s["proj_ev"], n[0])
            for i in range(3):
                for q in range(4):
                    last = tr(PS[0:6, i, 128 * q:128 * q + 128], cst[:, 4 * i + q, :])
                last.then_inc(s["cst_mm"], 1)
            pe.wait_ge(s["cso_ready"], 3)
            pe.wait_ge(s["t2_dve"], 9)
            pe.wait_ge(s["t2_act"], 3)

            def scores(i):
                t, hg, rows = i // 2, i % 2, ROWS[i // 2]
                if i >= 2:
                    pe.wait_ge(s["mx_ready"], i - 1)
                for h in range(4):
                    head = head_of(hg, h)
                    par = slice(64 * (head % 2), 64 * (head % 2) + 64)
                    q_ = qk[par, head // 2, HCOL[t]:HCOL[t] + rows]
                    o = PS[0:rows, 2 * (i % 2) + h // 2, :]
                    at0 = 256 * (h % 2)
                    if t < 2:
                        nk = 128 * (t + 1)
                        last = mm(o[:, at0:at0 + nk], q_, qk[par, 4 + head // 2, 0:nk], start=True, stop=True)
                    else:
                        mm(o[:, at0:at0 + PAST], q_, ckT[par, head // 2, :], start=True, stop=True)
                        last = mm(o[:, at0 + PAST:at0 + PAST + SS], q_,
                                  qk[par, 4 + head // 2, HCOL[2]:HCOL[2] + SS], start=True, stop=True)
                last.then_inc(s["qk_mm"], 1)

            scores(0)
            for i in range(6):
                t, hg, rows = i // 2, i % 2, ROWS[i // 2]
                if i < 5:
                    scores(i + 1)
                keys = ([128], [128, 128], [PAST, SS])[t]
                pe.wait_ge(s["exp_ready"], i + 1)
                if i:
                    pe.wait_ge(s["pT_ready"], i)
                for h in range(4):
                    for kk, nk in enumerate(keys):
                        c = len(keys) * h + kk
                        last = tr(PS[0:nk, 4 + c // 4, 128 * (c % 4):128 * (c % 4) + rows],
                                  sc[0:rows, h, 128 * kk:128 * kk + nk])
                last.then_inc(s["pT_mm"], 1)
                pe.wait_ge(s["pT_ready"], i + 1)
                if i:
                    pe.wait_ge(s["o_ready"], i)
                for h in range(4):
                    head = head_of(hg, h)
                    for kk, nk in enumerate(keys):
                        c = len(keys) * h + kk
                        if t == 2:
                            vals = (cv[:, :], vt[0:SS, 2, :])[kk]
                        else:
                            vals = vt[:, kk, :]
                        last = mm(PS[0:rows, 6, 64 * h:64 * h + 64], pT[0:nk, c, 0:rows],
                                  vals[:, 64 * head:64 * head + 64], start=(kk == 0), stop=(kk == len(keys) - 1))
                last.then_inc(s["pv_mm"], 1)
            for i in range(6):
                t, gg, rows = i // 2, i % 2, ROWS[i // 2]
                hc = slice(HCOL[t], HCOL[t] + rows)
                pe.wait_ge(s["dau_ready"], i + 1)
                if gg == 0:
                    if t:
                        pe.wait_ge(s["y_ev"], i)
                    if t == 2:
                        pe.wait_ge(s["sraw_ev"], 2)
                    mm(PS[0:rows, 0, 0:16], upper[0:rows, 0:rows], dA[0:rows, t, :], start=True, stop=True)
                    mm(PS[0:rows, 0, 16:32], lower[0:rows, 0:rows], dA[0:rows, t, :], start=True, stop=True)
                    mm(PS[:, 0, 32:48], ones[0:rows, :], dA[0:rows, t, :], start=True, stop=True)\
                        .then_inc(s["cum_mm"], 1)
                    for q in range(2):
                        last = mm(PS[0:rows, 1, 128 * q:128 * q + rows], conv[:, XT + q, hc], conv[:, XT + 2 + q, hc],
                                  start=True, stop=True)
                    last.then_inc(s["gt_mm"], 1)
                if i:
                    pe.wait_ge(s["seg_exp"], i)
                for q in range(2):
                    last = mm(PS[0:rows, 2 + q, 0:4 * rows], lower[0:rows, 0:rows], dau[0:rows, 4 * q:4 * q + 4, 0:rows],
                              start=True, stop=True)
                last.then_inc(s["seg_mm"], 1)
                pe.wait_ge(s["xw_ready"], i + 1)
                pe.wait_ge(s["m_ready"], i + 1)
                if i:
                    pe.wait_ge(s["y_ev"], i)
                for h in range(8):
                    mm(PS[0:rows, 4, 64 * h:64 * h + 64], ee[0:rows, h, 0:rows], xdt[0:rows, h, :], start=True, stop=True)
                if t:
                    mm(PS[0:rows, 5, :], conv[:, XT + 2 + gg, hc], hst[:, 512 * gg:512 * gg + 512], start=True, stop=True)
                mm(PS[:, 6, :], bt[0:rows, t, 128 * gg:128 * gg + 128], xw[0:rows].rearrange("p h d -> p (h d)"),
                   start=True, stop=True).then_inc(s["y_mm"], 1)
                if i in (3, 5):
                    pe.wait_ge(s["y_ev"], i + 1)
                    for q in range(2):
                        for c in range(4):
                            last = tr(PS[:, (7, 1)[q], 128 * c:128 * c + 128], hst[:, 512 * q + 128 * c:512 * q + 128 * c + 128])
                        last.then_inc(s["hst_mm"], 1)
                if i == 3:
                    pe.wait_ge(s["sraw_in"], 16)
                    for q in range(2):
                        pe.wait_ge(s["hst_ev"], q + 1)
                        for c in range(4):
                            last = tr(PS[:, (7, 1)[q], 128 * c:128 * c + 128], s_raw[:, 4 * q + c, :])
                        last.then_inc(s["sraw_mm"], 1)
            for i in range(9):
                t, q, rows = i // 3, i % 3, ROWS[i // 3]
                pe.wait_ge(s["mixn"], i + 1)
                if i >= 4:
                    pe.wait_ge(s["mixT_ready"], i - 3)
                for c in range(4):
                    src = z[0:rows, t, 512 * q + 128 * c:512 * q + 128 * c + 128] if q < 2 else \
                        ot[0:rows, t, 128 * c:128 * c + 128]
                    last = tr(PS[:, i % 4, 128 * c:128 * c + rows], src)
                last.then_inc(s["mixT_mm"], 1)
            for i in range(6):
                t, h, rows = i // 2, i % 2, ROWS[i // 2]
                pe.wait_ge(s["mixT_ready"], 3 * t + 3)
                if i == 0:
                    pe.wait_ge(s["hst_ev"], 4)
                    for j in range(N_OUT):
                        pe.wait_ge(w_full[slot_of(N_IN + j)], 16 * ((N_IN + j) // SLOTS + 1))
                if i >= 4:
                    pe.wait_ge(s["x1_ready"], i - 3)
                for k in range(MT):
                    w = ring[:, slot_of(N_IN + k // 4), :].rearrange("p (k n) -> p k n", k=4)
                    last = mm(PS[0:rows, 4 + i % 4, :], mixT[:, k, TCOL[t]:TCOL[t] + rows],
                              w[:, k % 4, 512 * h:512 * h + 512], start=(k == 0), stop=(k == MT - 1))
                last.then_inc(s["out_mm"], 1)
            for i in range(6):
                t, h, rows = i // 2, i % 2, ROWS[i // 2]
                pe.wait_ge(s["xn_ready"], t + 1)
                if i >= 4:
                    pe.wait_ge(s["hf_ready"], i - 3)
                for c in range(4):
                    last = tr(PS[:, i % 4, 128 * c:128 * c + rows], xn[0:rows, t, 512 * h + 128 * c:512 * h + 128 * c + 128])
                last.then_inc(s["hf_mm"], 1)
            pe.wait_ge(s["hf_ready"], 6)
            pe.wait_ge(s["x1_ready"], 6)
            for k in range(KD):
                last = mm(PS[0:NE, 4, 0:TC], wr[:, k, :], hfT[:, k, :], start=(k == 0), stop=(k == KD - 1))
            last.then_inc(s["lg_mm"], 1)
            pe.wait_ge(s["lgT_ready"], 1)
            for t in range(NT):
                last = tr(PS[0:ROWS[t], 5, 32 * t:32 * t + 32], lgT[:, TCOL[t]:TCOL[t] + ROWS[t]])
            last.then_inc(s["lgt_mm"], 1)
            pe.wait_ge(s["rexp"], 2)
            for t in range(NT + 1):
                cols = slice(32 * t, 32 * t + 32)
                rows = ROWS[t] if t < NT else 128
                for u in range(min(t, NT - 1) + 1):
                    k = ROWS[u]
                    lhs = strict[0:k, 0:rows] if u == t else ones[0:k, 0:rows]
                    last = mm(PS[0:rows, 6, cols], lhs, chosen[0:k, u, :], start=(u == 0), stop=(u == min(t, NT - 1)))
            last.then_inc(s["pos_mm"], 1)

            pe.wait_ge(s["bej_ready"], 1)
            for c in range(2):
                last = tr(PS[0:1, 7, 128 * c:128 * c + 128], bej[:, c:c + 1])
            last.then_inc(s["bej_mm"], 1)

            def gather(b):
                pe.wait_ge(s["p_ready"], 3 * b + 3)
                for t in range(NT):
                    for h in range(2):
                        last = mm(PS[64 * h:64 * h + 64, 3, :], pm[:, t, 64 * h:64 * h + 64],
                                  xn[:, t, 512 * h:512 * h + 512], start=(t == 0), stop=(t == NT - 1))
                last.then_inc(s["xe_mm"], 1)
                pe.wait_ge(s["c_ready"], b + 1)
                for t in range(NT):
                    last = tr(PS[:, 5, 128 * t:128 * t + 128], pm[:, t, :])
                last.then_inc(s["ct_mm"], 1)

            def turn(b):
                pe.wait_ge(s["xe_ev"], b + 1)
                for c in range(4):
                    last = tr(PS[:, 3, 128 * c:128 * c + 128], xe[:, 128 * c:128 * c + 128])
                last.then_inc(s["xt_mm"], 1)

            def combine(b):
                pe.wait_ge(s["yy_ready"], b + 2)
                pe.wait_ge(s["yyl_ready"], b + 2)
                pe.wait_ge(s["c_ready"], b + 2)
                for i in range(6):
                    t, h = i // 2, i % 2
                    pe.wait_ge(s["o_ev"], 6 * (b + 1) + i + 1)
                    for part in range(2):
                        last = mm(PS[0:ROWS[t], 6 + h, :], c01[:, h, TCOL[t]:TCOL[t] + ROWS[t]], yy2[:, part, :],
                                  start=(part == 0), stop=(part == 1))
                    last.then_inc(s["comb_mm"], 1)

            pe.wait_ge(s["route_ready"], 1)
            total = pe.value_load(blocks[0:1, 0:1], min_val=NE, max_val=MAX_BLOCKS)
            gather(0)
            turn(0)
            with pe.Fori(0, total) as b:
                e = pe.value_load(expert_of[0:1, bass.ds(b, 1)], min_val=0, max_val=NE - 1)
                pe.wait_ge(s["xt_ev"], b + 1)
                pe.wait_ge(s["sel_ready"], b + 1)
                pe.wait_ge(s["gu_ev"], b + 1)
                for m in range(2):
                    for part in range(2):
                        mm(bank(m), sel[:, 2 * m:2 * m + 2, :], b_gu2[:, part, :], start=(part == 0), stop=False)
                for c in range(GU_CHUNKS):
                    if c == 1:
                        combine(b - 1)
                    pe.wait_ge(w_full[slot_of(FRONT + c)], 16 * ((FRONT + c) // SLOTS + 1) + 16 * e)
                    w = ring[:, slot_of(FRONT + c), :].rearrange("p (k n) -> p k n", k=2)
                    for kk in range(2):
                        k = 2 * c + kk
                        for m in range(2):
                            for h in range(2):
                                last = mm(PS[64 * h:64 * h + 64, m, :], xt[:, k % 4, k // 4, :],
                                          w[:, kk, D * m + 512 * h:D * m + 512 * h + 512],
                                          start=False, stop=(k == KD - 1))
                    last.then_inc(s[("gs_used", "gs_used1", "gs_used2", "gu_mm")[c]], 1)
                gather(b + 1)
                pe.wait_ge(s["act_ready"], 2 * b + 2)
                pe.wait_ge(s["at_ev"], b + 1)
                for c in range(4):
                    last = tr(PS[:, 4, 128 * c:128 * c + 128], ac[:, 128 * c:128 * c + 128])
                last.then_inc(s["at_mm"], 1)
                turn(b + 1)
                pe.wait_ge(s["seld_ready"], b + 1)
                for part in range(2):
                    mm(bank(2), sel_dn[:, :, :], b_dn2[:, part, :], start=(part == 0), stop=False)
                pe.wait_ge(s["at_ev"], b + 2)
                for c in range(DN_CHUNKS):
                    i = FRONT + GU_CHUNKS + c
                    pe.wait_ge(w_full[slot_of(i)], 16 * (i // SLOTS + 1) + 16 * e)
                    w = ring[:, slot_of(i), :].rearrange("p (k n) -> p k n", k=4)
                    for kk in range(4):
                        for h in range(2):
                            last = mm(PS[64 * h:64 * h + 64, 2, :], at[:, kk, c, :],
                                      w[:, kk, 512 * h:512 * h + 512], start=False,
                                      stop=(c == 1 and kk == 3))
                    last.then_inc(s[("ds_used", "d_mm")[c]], 1)
            combine(total - 1)


def head_of(group, n):
    return 4 * group + 2 * (n % 2) + n // 2


def backwards(v, at, n):
    return v[:, :, at:at - n:-1] if at >= n else v[:, :, at::-1]


def seg_ps(PS, rows):
    v = PS[0:rows, 2:4, 0:4 * rows]
    return v.rearrange("p b (h n) -> p b h n", n=rows)


def dau_flat(r6, rows):
    return r6[0:rows, 0:512]


_INS = ['x_prompt', 'x_sample', 'cache_k', 'cache_v', 'state_conv', 'state_ssm',
        'norm_mix_g', 'w_in', 'conv_w', 'conv_b', 'dt_bias', 'a_log', 'd_skip', 'ssm_norm_g',
        'att_norm_g', 'rel_bias_table', 'w_out', 'norm_ffn_g', 'w_router', 'b_router',
        'w_gate_up', 'b_gate_up', 'w_down', 'b_down', 'norm_final_g']
_OUTS = [(1, SP, D), (1, SS, D), (1, 1, SP, AH, AD), (1, 1, SP, AH, AD), (1, 1, TAPS - 1, D_CONV),
         (1, 1, HEADS, P_HEAD, NSTATE), (1, 1, SS, AH, AD), (1, 1, SS, AH, AD), (1, 1, TAPS - 1, D_CONV),
         (1, 1, HEADS, P_HEAD, NSTATE)]


def kernel(**inputs):
    import numpy as _np
    import concourse.bacc as _bacc
    from concourse import mybir as _mybir
    from concourse.bass_utils import run_bass_kernel_spmd as _run

    nc = _bacc.Bacc("TRN2", target_bir_lowering=False, num_devices=1)
    arrays, args = {}, []
    for name in _INS:
        a = _np.ascontiguousarray(inputs[name])
        arrays[f"in_{name}_dram"] = a
        args.append(nc.dram_tensor(f"in_{name}_dram", a.shape, _mybir.dt.from_np(a.dtype), kind="ExternalInput").ap())
    for i, shape in enumerate(_OUTS):
        args.append(nc.dram_tensor(f"out_{i}_dram", shape, _mybir.dt.float32, kind="ExternalOutput").ap())
    build(nc, *args)
    r = _run(nc, [arrays], core_ids=[0])
    return tuple(r.results[0][f"out_{i}_dram"] for i in range(len(_OUTS)))
```

```python
import numpy as np
import concourse.bass as bass
from concourse import mybir
from contextlib import ExitStack

D = 1024
SP, SS = 256, 64
HEADS, P_HEAD, NSTATE, GROUPS = 16, 64, 128, 2
D_SSM = HEADS * P_HEAD
D_CONV = D_SSM + 2 * GROUPS * NSTATE
TAPS = 4
AH, AD = 8, 64
D_ATT = AH * AD
D_MIX = D_SSM + D_ATT
PAST = 128
CLIP = 128
NREL = 2 * CLIP + 1
NE, TOPK, F = 32, 4, 1024
EPS = 1e-5
ALPHA, LIMIT = 1.702, 7.0
NEG = -1.0e30

ROWS = [128, 128, 64]
NT = 3
HCOL = [0, 128, 259]
HC = 323
TCOL = [0, 128, 256]
TC = 320
KD = D // 128
CT = D_CONV // 128
XT = D_SSM // 128
MT = D_MIX // 128
SLOTS, SLOT = 6, 4096
FRONT_SLOTS = 5
CAP = 64
HALF = 512

C_Z, C_XBC, C_DT = 0, D_SSM, D_SSM + D_CONV
C_Q = C_DT + HEADS
W_IN_CHUNKS = [C_XBC, C_XBC + 512, C_XBC + 1024, C_Q, C_Q + 512, C_Q + 1024, C_Z, C_Z + 512]
N_IN, N_OUT = len(W_IN_CHUNKS), 3
FRONT = N_IN + N_OUT
GU_CHUNKS, DN_CHUNKS = 4, 2
EXPERT_SLOT = (1, 2, 3, 4, 0, 5)
N_SMALL = 21
MAX_BLOCKS = NE + TC * TOPK // CAP


def build(nc, x_prompt, x_sample, cache_k, cache_v, state_conv, state_ssm,
          norm_mix_g, w_in, conv_w, conv_b, dt_bias, a_log, d_skip, ssm_norm_g,
          att_norm_g, rel_bias_table, w_out, norm_ffn_g, w_router, b_router,
          w_gate_up, b_gate_up, w_down, b_down, norm_final_g,
          y_prompt, y_sample, k_prompt, v_prompt, conv_prompt, ssm_prompt,
          k_sample, v_sample, conv_sample, ssm_sample):
    f32, i32, u32, f32r = mybir.dt.float32, mybir.dt.int32, mybir.dt.uint32, mybir.dt.float32r
    ALU = mybir.AluOpType
    ACT = mybir.ActivationFunctionType
    X = mybir.AxisListType.X
    ctx = ExitStack()
    with ctx:
        def sb(name, shape, dt=f32):
            return ctx.enter_context(nc.sbuf_tensor(name, shape, dt))

        def sem(name):
            return ctx.enter_context(nc.semaphore(name))

        ring = sb("ring", [128, SLOTS, SLOT])
        r1 = sb("r1", [128, 3072])
        r2 = sb("r2", [128, 2584])
        r3 = sb("r3", [128, 3912])
        r4 = sb("r4", [128, 3876])
        r5 = sb("r5", [128, 2584])
        r6 = sb("r6", [128, 4096])
        with ExitStack() as early:
            def sb_early(name, shape):
                return early.enter_context(nc.sbuf_tensor(name, shape, f32))

            e1 = sb_early("e1", [128, 1536])
            ot = sb_early("ot", [128, NT, D_ATT])
            e2 = sb_early("e2", [128, 1536])
        b_gu2 = sb("b_gu2", [128, 2, HALF], f32r)
        b_dn2 = sb("b_dn2", [128, 2, HALF], f32r)
        yy2 = sb("yy2", [128, 2, HALF], f32r)
        c01 = sb("c01", [128, 2, TC], f32r)
        sel = sb("sel", [128, 4, CAP], f32r)
        sel_dn = sb("sel_dn", [128, 2, CAP], f32r)
        lg = sb("lg", [128, NT, NE])
        one = sb("one", [128, NT, NE])
        chosen = sb("chosen", [128, NT, NE])
        pg = sb("pg", [128, NE, 2 * NT])
        pcur = sb("pcur", [128, 2 * NT])
        gprev = sb("gprev", [128, NT])
        nbk = sb("nbk", [128, 4, NE])
        bej = sb("bej", [128, 2])
        before = sb("before", [1, NE], i32)
        blocks = sb("blocks", [1, 1], i32)
        expert_of = sb("expert_of", [1, 128], i32)
        place_of = sb("place_of", [1, 128], i32)

        def view(region, at, *dims):
            n = int(np.prod(dims))
            v = region[:, at:at + n]
            if len(dims) == 2:
                return v.rearrange("p (a b) -> p a b", b=dims[1])
            if len(dims) == 3:
                return v.rearrange("p (a b c) -> p a b c", b=dims[1], c=dims[2])
            return v

        x = view(r1, 0, NT, D)
        z = view(r1, 0, NT, D)
        hT = view(r2, 0, KD, HC)
        kt = ring[:, SLOTS - 1, 0:NT * D_ATT].rearrange("p (t n) -> p t n", n=D_ATT)
        s_out = view(r2, 1536, 8, NSTATE)
        pad = view(r3, 0, CT, HC + 3)
        xs = view(r3, 0, NT, D)
        bt = view(r3, 3072, NT, 256)
        xn = view(r3, 0, NT, D)
        praw = r4[0:88, 0:128]
        eq = r4[:, 0:NT * TOPK * NE].rearrange("p (t k e) -> p t k e", k=TOPK, e=NE)
        conv = view(r4, 0, CT, HC)
        mixT = ring[:, SLOTS - 1, 0:MT * TC].rearrange("p (k n) -> p k n", n=TC)
        qk = view(r5, 0, 8, HC)
        hst = view(r5, 0, D_SSM)
        hst_s = view(r5, 1024, D_SSM)
        acc = view(r5, 2048, 8, P_HEAD)
        vt = view(e1, 0, NT, D_ATT)
        s_raw = view(e1, 0, 8, NSTATE)
        ck = view(e2, 0, D_ATT)
        cv = view(e2, 512, D_ATT)
        ckT = view(e2, 1024, 4, PAST)
        hraw = view(r6, 0, D_CONV)
        tab = r6[0:AH, 1536:1536 + NREL]
        ext = r6[0:AH, 1800:2183]
        iota_i = r6[:, 2200:2200 + TC].bitcast(i32)
        pidx_i = r6[:, 2199:2200].bitcast(i32)
        dtT = r6[0:HEADS, 2624:2624 + HC]
        bias = view(r6, 0, AH, 256)
        sc = view(r6, 2048, 4, 256)
        pT = view(r6, 3072, 8, 128)
        cso = view(r6, 2048, D_CONV)
        scratch = view(r6, 3072, D)
        sq = view(r2, 0, HALF)
        dau = view(r6, 0, 8, 128)
        ee2 = (view(r6, 1024, 8, 128), view(e2, 0, 8, 128))
        xdt2 = (view(r6, 2048, 8, P_HEAD), view(e2, 1024, 8, P_HEAD))
        xw2 = (view(r6, 2560, 8, P_HEAD), view(e1, 1024, 8, P_HEAD))
        yo = view(r6, 3072, 8, P_HEAD)
        gm = view(r6, 3584, GROUPS, 128)
        hfT = view(r6, 0, KD, TC)
        xe = view(r6, 0, HALF)
        xt = view(r6, 512, 4, 2, CAP)
        ug = view(r6, 1024, HALF)
        sg = view(r6, 1536, HALF)
        uu = view(r6, 2048, HALF)
        ac = view(r6, 2560, HALF)
        at = view(r6, 3072, 4, 2, CAP)
        pm = view(r2, 0, NT, 128)
        gfin = view(r2, 1536, D)

        b_gu = sb("b_gu", [128, HALF])
        b_dn = sb("b_dn", [128, HALF])
        ident = sb("ident", [128, 128])
        upper = sb("upper", [128, 128])
        strict = sb("strict", [128, 128])
        lower = sb("lower", [128, 128])
        ones = sb("ones", [128, 128])
        iota = sb("iota", [128, TC])
        prevT = sb("prevT", [128, CT, 3])
        cst = sb("cst", [128, CT, 6])
        par = sb("par", [128, 88])
        gmix, gffn, gout, cb = par[:, 0:8], par[:, 8:16], par[:, 16:28], par[:, 28:40]
        cw = par[:, 40:88].rearrange("p (j c) -> p c j", j=TAPS)
        wdt = sb("wdt", [128, KD, HEADS])
        wr = sb("wr", [128, KD, NE])
        brt = sb("brt", [128, NE])
        dtb = sb("dtb", [128, HEADS])
        alog = sb("alog", [128, HEADS])
        dsk = sb("dsk", [128, HEADS])
        dta = sb("dta", [128, NT, HEADS])
        dtt = sb("dtt", [128, NT, HEADS])
        dt = sb("dt", [128, NT, HEADS])
        dA = sb("dA", [128, NT, HEADS])
        edec = sb("edec", [128, NT, 48])
        stat = sb("stat", [128, 24])
        mx = sb("mx", [128, 4])
        sm = sb("sm", [128, 4])
        rs = sb("rs", [128, 4])
        m8 = sb("m8", [128, NT, 8])
        i8 = sb("i8", [128, NT, 8], u32)
        ix = sb("ix", [128, NT, 8])
        pv = sb("pv", [128, NT, 4])
        ps4 = sb("ps4", [128, NT])
        pidx = sb("pidx", [128, 1])
        PS = ctx.enter_context(nc.psum_tensor("PS", [128, 8, 512], f32))
        table_d = nc.dram_tensor("bias_table_clipped", (AH, 383), f32)

        names = """consts par_mm par_ready x_in small_in cvhist_in ext_out bias_in sraw_in gfin_in ssq rstd xnorm
            hT_mm hT_ready hist_mm ck_mm ck_ready proj_mm proj_ev conv_done silu_done t2_mm t2_dve t2_act
            dtc_ready ln_done cst_ready cst_mm cso_ready cso_out ktv_out qk_mm mx_ready exp_ready pT_mm
            pT_ready pv_mm o_ready dau_ready seg_mm seg_exp gt_mm gm_ready ed_ready m_ready xw_ready y_mm
            y_ev hst_mm hst_ev sraw_mm sraw_ev sout_out sqrt2 mixn mixT_mm mixT_ready out_mm x1_ready sqrt3
            xn_ready hf_mm hf_ready lgt_mm rexp pv_ready pos_mm route_ready p_ready xe_mm ct_mm xe_ev xt_mm
            xt_ev gu_mm gs_used gs_used1 gs_used2 ds_used g_ready gu_ev sig_ready act_ready comb_mm o_ev
            c_ready at_mm at_ev d_mm yy_ready z_mm z_ev z_silu yb_free rec2 bej_ready bej_mm b_hi yyl_ready
            sel_ready seld_ready pcur_ready gates_held sqrt4 fin_ready y_out vchain achain pchain""".split()
        s = {n: sem(n) for n in names}
        xres_in = [sem(f"xres_in{t}") for t in range(NT)]
        w_full = [sem(f"w_full{i}") for i in range(SLOTS)]
        block = ctx.enter_context(nc.Block())

        def bank(b, rows=128):
            return PS[0:rows, b, :]

        def bc(ap, *shape):
            return ap.to_broadcast(list(shape))

        def slot_of(chunk):
            return chunk % FRONT_SLOTS

        def front_arrival(chunk):
            return 16 * (chunk // FRONT_SLOTS + 1)

        def expert_arrival(c):
            return 16 * (len(range(EXPERT_SLOT[c], FRONT, FRONT_SLOTS)) if EXPERT_SLOT[c] < FRONT_SLOTS else 0) + 16

        @block.sync
        def _(sp):
            def load(slot, k, src):
                sp.dma_start(ring[:, slot, :].rearrange("p (k n) -> p k n", k=k), src).then_inc(w_full[slot], 16)

            def wait_used(i):
                if i < 6:
                    sp.wait_ge(s["proj_mm"], 4 * i + 4 if i < 5 else 21 + NT)
                elif i < N_IN:
                    sp.wait_ge(s["z_mm"], NT * (i - 5))
                else:
                    sp.wait_ge(s["out_mm"], 2 * NT)

            for t in range(2):
                sp.dma_start(x[:, t, :], x_prompt[0, 128 * t:128 * t + 128, :]).then_inc(s["x_in"], 16)
            sp.dma_start(x[0:SS, 2, :], x_sample[0, :, :]).then_inc(s["x_in"], 16)
            sp.wait_ge(s["x_in"], 48)
            sp.wait_ge(s["small_in"], N_SMALL * 16)
            w3 = w_in[0].rearrange("(k p) n -> p k n", p=128)
            for i, c in enumerate(W_IN_CHUNKS):
                if i >= FRONT_SLOTS:
                    wait_used(i - FRONT_SLOTS)
                load(slot_of(i), KD, w3[:, :, c:c + 512])
            wo = w_out[0].rearrange("(k p) n -> p k n", p=128)
            for j in range(N_OUT):
                wait_used(N_IN + j - FRONT_SLOTS)
                load(slot_of(N_IN + j), 4, wo[:, 4 * j:4 * j + 4, :])

            def load_expert(e, c):
                if c < GU_CHUNKS:
                    w, k0, k = w_gate_up[0], 2 * c, 2
                else:
                    w, k0, k = w_down[0], 4 * (c - GU_CHUNKS), 4
                load(EXPERT_SLOT[c], k, w[bass.ds(e, 1)].rearrange("a (k p) n -> p (a k) n", p=128)[:, k0:k0 + k, :])

            for c in range(GU_CHUNKS + DN_CHUNKS):
                slot = EXPERT_SLOT[c]
                wait_used(max(range(slot, FRONT, FRONT_SLOTS)) if slot < FRONT_SLOTS else N_IN)
                load_expert(0, c)
            sp.wait_ge(s["route_ready"], 1)
            used = ["gs_used", "gs_used1", "gs_used2", "gu_mm", "ds_used", "d_mm"]
            with sp.Fori(1, NE) as e:
                first = sp.value_load(before[0:1, bass.ds(e, 1)], min_val=1, max_val=MAX_BLOCKS)
                for c in range(GU_CHUNKS + DN_CHUNKS):
                    sp.wait_ge(s[used[c]], first)
                    load_expert(e, c)
            for t in range(2):
                sp.wait_ge(s["fin_ready"], t + 1)
                sp.dma_start(y_prompt[0, 128 * t:128 * t + 128, :], xn[:, t, :]).then_inc(s["y_out"], 16)
            sp.wait_ge(s["fin_ready"], 3)
            sp.dma_start(y_sample[0, :, :], xn[0:SS, 2, :]).then_inc(s["y_out"], 16)
            sp.wait_ge(s["y_out"], 48)
            sp.wait_ge(s["ktv_out"], 6 * 16)
            sp.wait_ge(s["cso_out"], 2 * 16)
            sp.wait_ge(s["sout_out"], 2 * 16)

        @block.gpsimd
        def _(pool):
            g = nc.gpsimd
            npc = [0]

            def step(ins):
                npc[0] += 1
                ins.then_inc(s["pchain"], 1)
                pool.wait_ge(s["pchain"], npc[0])

            for m in (upper, strict, lower, ident, ones):
                step(g.memset(m[:, :], 0.0 if m is ident else 1.0))
            step(g.affine_select(out=ident[:, :], in_=ident[:, :], compare_op=ALU.not_equal, fill=1.0,
                                 base=0, pattern=[[-1, 128]], channel_multiplier=1))
            step(g.affine_select(out=upper[:, :], in_=upper[:, :], compare_op=ALU.is_ge, fill=0.0,
                                 base=0, pattern=[[1, 128]], channel_multiplier=-1))
            step(g.affine_select(out=strict[:, :], in_=strict[:, :], compare_op=ALU.is_gt, fill=0.0,
                                 base=0, pattern=[[1, 128]], channel_multiplier=-1))
            step(g.affine_select(out=lower[:, :], in_=lower[:, :], compare_op=ALU.is_gt, fill=0.0,
                                 base=0, pattern=[[-1, 128]], channel_multiplier=1))
            step(g.iota(iota_i, pattern=[[1, TC]], base=0, channel_multiplier=0))
            step(g.tensor_copy(iota[:, :], iota_i))
            step(g.iota(pidx_i, pattern=[[0, 1]], base=0, channel_multiplier=1))
            step(g.tensor_copy(pidx[:, :], pidx_i))
            step(g.memset(b_dn[64:128, :], 0.0))
            step(g.memset(pad[:, :, 0:3], 0.0))
            step(g.memset(hT[:, :, 256:259], 0.0))
            g.memset(stat[:, :], 1.0).then_inc(s["consts"], 1)

            for t in range(NT):
                rows = ROWS[t]
                kd = k_prompt[0, 0, 128 * t:128 * t + 128] if t < 2 else k_sample[0, 0]
                vd = v_prompt[0, 0, 128 * t:128 * t + 128] if t < 2 else v_sample[0, 0]
                pool.wait_ge(s["t2_act"], t + 1)
                pool.dma_start(kd.rearrange("n h d -> n (h d)"), kt[0:rows, t, :]).then_inc(s["ktv_out"], 16)
                pool.dma_start(vd.rearrange("n h d -> n (h d)"), vt[0:rows, t, :]).then_inc(s["ktv_out"], 16)
            pool.wait_ge(s["cso_ready"], 3)
            pool.dma_start(conv_prompt[0, 0], cso[0:3, :]).then_inc(s["cso_out"], 16)
            pool.dma_start(conv_sample[0, 0], cso[3:6, :]).then_inc(s["cso_out"], 16)
            pool.wait_ge(s["ktv_out"], 6 * 16)
            pool.wait_ge(s["pv_mm"], 6)
            pool.dma_start(s_raw, state_ssm[0, 0].rearrange("(c a) p n -> (a p) c n", a=2)).then_inc(s["sraw_in"], 16)
            for n, dst in enumerate((ssm_prompt, ssm_sample)):
                pool.wait_ge(s["hst_ev"], 2 * n + 2)
                pool.dma_start(dst[0, 0].rearrange("(c a) p n -> (a p) c n", a=2), s_out).then_inc(s["sout_out"], 16)
            for t in range(NT):
                pool.wait_ge(s["mixT_mm"], 3 * t + 3)
                src = x_prompt[0, 128 * t:128 * t + 128, :] if t < 2 else x_sample[0, :, :]
                pool.dma_start(x[0:ROWS[t], t, :], src).then_inc(xres_in[t], 16)
            pool.wait_ge(s["ktv_out"], 6 * 16)
            pool.wait_ge(s["sout_out"], 2 * 16)
            pool.dma_start(gfin, norm_final_g.rearrange("(a n) -> a n", a=1).to_broadcast([128, D])).then_inc(s["gfin_in"], 16)

        @block.scalar
        def _(act):
            a = nc.scalar
            ac_n = [0]

            def step(ins):
                ac_n[0] += 1
                ins.then_inc(s["achain"], 1)
                act.wait_ge(s["achain"], ac_n[0])

            def small(dst, src):
                act.dma_start(dst, src).then_inc(s["small_in"], 16)

            for at0, src in ((0, norm_mix_g[0]), (8, norm_ffn_g[0]), (16, ssm_norm_g[0]), (24, att_norm_g[0]), (28, conv_b[0])):
                k = src.shape[0] // 128
                small(praw[at0:at0 + k, :], src.rearrange("(k p) -> k p", p=128))
            small(praw[40:88, :], conv_w[0].rearrange("j (k p) -> (j k) p", p=128))
            small(brt[:, :], b_router[0:1, :].to_broadcast([128, NE]))
            small(dtb[:, :], dt_bias[0:1, :].to_broadcast([128, HEADS]))
            small(alog[:, :], a_log[0:1, :].to_broadcast([128, HEADS]))
            small(dsk[:, :], d_skip[0:1, :].to_broadcast([128, HEADS]))
            small(tab[:, :], rel_bias_table[0])
            small(wr[:, :, :], w_router[0].rearrange("(k p) n -> p k n", p=128))
            small(wdt[:, :, :], w_in[0].rearrange("(k p) n -> p k n", p=128)[:, :, C_DT:C_DT + HEADS])
            small(ck[:, :], cache_k[0, 0].rearrange("n h d -> n (h d)"))
            small(cv[:, :], cache_v[0, 0].rearrange("n h d -> n (h d)"))
            for c in range(4):
                small(b_gu[32 * c:32 * c + 32, :], b_gate_up[0][:, 512 * c:512 * c + 512])
            for c in range(2):
                small(b_dn[32 * c:32 * c + 32, :], b_down[0][:, 512 * c:512 * c + 512])
            act.dma_start(hraw[0:3], state_conv[0, 0]).then_inc(s["cvhist_in"], 16)
            act.wait_ge(s["consts"], 1)
            act.wait_ge(s["x_in"], 48)
            for t in range(NT):
                step(a.activation(scratch[0:ROWS[t]], x[0:ROWS[t], t, :], ACT.Square,
                                  accum_out=stat[0:ROWS[t], t:t + 1]))
            a.activation(stat[:, 3:6], stat[:, 0:3], ACT.Copy).then_inc(s["ssq"], 1)
            act.wait_ge(s["rstd"], 1)
            a.activation(stat[:, 0:3], stat[:, 3:6], ACT.Sqrt).then_inc(s["ssq"], 1)
            act.wait_ge(s["ext_out"], 1)
            act.dma_start(table_d.ap(), ext[:, :]).then_inc(s["ext_out"], 16)
            act.wait_ge(s["ext_out"], 17)
            act.wait_ge(s["hist_mm"], 1)
            for q in range(4):
                act.dma_start(bias[:, 2 * q:2 * q + 2, :], bass.AP(
                    table_d, head_of(q // 2, 2 * (q % 2)) * 383, [[1, 128], [2 * 383, 2], [1, 256]]))\
                    .then_inc(s["bias_in"], 16)

            def out_of(n, dst, src, func=ACT.Copy):
                act.wait_ge(s["proj_mm"], n + 1)
                a.activation(dst, src, func).then_inc(s["proj_ev"], 1)

            def copy_rows(dst, t, cols, b):
                if t < 2:
                    return a.activation(dst[:, t, cols], PS[:, b, :], ACT.Copy)
                for q in range(2):
                    last = a.activation(dst[0:SS, t, cols.start + 256 * q:cols.start + 256 * q + 256],
                                        PS[64 * q:64 * q + 64, b, 0:256], ACT.Copy)
                return last

            n = 0
            for c in range(CT):
                out_of(n, pad[:, c, 3:3 + HC], PS[:, n % 4, 0:HC])
                n += 1
            for c in range(8):
                out_of(n, qk[:, c, :], PS[:, n % 4, 0:HC])
                n += 1
            out_of(n, dtT[:, :], PS[0:HEADS, n % 4, 0:HC])
            n += 1
            for t in range(NT):
                act.wait_ge(s["proj_mm"], n + 1)
                copy_rows(vt, t, slice(0, 512), n % 4).then_inc(s["proj_ev"], 1)
                n += 1
            for c in range(3):
                act.wait_ge(s["conv_done"], 4 * c + 4)
                a.activation(conv[:, 4 * c:4 * c + 4, :], conv[:, 4 * c:4 * c + 4, :], ACT.Silu)\
                    .then_inc(s["silu_done"], 1)
            act.wait_ge(s["dtc_ready"], 1)
            step(a.activation(alog[:, :], alog[:, :], ACT.Exp))
            step(a.activation(dtt[:, :, :], dta[:, :, :], ACT.Exp, scale=-1.0))
            a.activation(dtt[:, :, :], dtt[:, :, :], ACT.Ln, bias=1.0).then_inc(s["ln_done"], 1)
            for t in range(NT):
                act.wait_ge(s["t2_mm"], 3 * t + 4)
                a.activation(kt[0:ROWS[t], t, :], PS[0:ROWS[t], 7, :], ACT.Copy).then_inc(s["t2_act"], 1)
            for i in range(6):
                t, rows = i // 2, ROWS[i // 2]
                nk = (128, 256, PAST + SS)[t]
                act.wait_ge(s["mx_ready"], i + 1)
                for h in range(4):
                    last = a.activation(sc[0:rows, h, 0:nk], sc[0:rows, h, 0:nk], ACT.Exp,
                                        bias=mx[0:rows, h:h + 1], accum_out=sm[0:rows, h:h + 1])
                last.then_inc(s["exp_ready"], 1)
                h, t = i // NT, i % NT
                act.wait_ge(s["z_mm"], i + 1)
                copy_rows(z, t, slice(512 * h, 512 * h + 512), 7).then_inc(s["z_ev"], 1)

            def norm_mixed(t):
                rows = ROWS[t]
                parts = [z[0:rows, t, 512 * gg:512 * gg + 512] for gg in range(GROUPS)] + [ot[0:rows, t, :]]
                ss = stat[0:rows, 12 + 3 * t:15 + 3 * t]
                act.wait_ge(s["y_ev"], 2 * t + 2)
                for q in range(3):
                    step(a.activation(sq[0:rows], parts[q], ACT.Square, accum_out=ss[:, q:q + 1]))
                a.activation(ss, ss, ACT.Sqrt, scale=1.0 / 512, bias=stat[0:rows, 10:11]).then_inc(s["sqrt2"], 1)
                act.wait_ge(s["rec2"], t + 1)
                for q in range(3):
                    a.activation(parts[q], parts[q], ACT.Identity, scale=ss[:, q:q + 1]).then_inc(s["mixn"], 1)

            def mixed_out(t):
                rows = ROWS[t]
                for q in range(3):
                    act.wait_ge(s["mixT_mm"], 3 * t + q + 1)
                    for c in range(4):
                        last = a.activation(mixT[:, 4 * q + c, TCOL[t]:TCOL[t] + rows],
                                            PS[:, mix_bank(3 * t + q), 128 * c:128 * c + rows], ACT.Identity,
                                            scale=gout[:, 4 * q + c:4 * q + c + 1])
                    last.then_inc(s["mixT_ready"], 1)

            act.wait_ge(s["ktv_out"], 6 * 16)
            for i in range(6):
                t, rows = i // 2, ROWS[i // 2]
                if i % 2 == 0:
                    act.wait_ge(s["gt_mm"], t + 1)
                    a.activation(edec[0:rows, t, 0:32], PS[0:rows, 0, 0:32], ACT.Exp)
                    a.activation(edec[:, t, 32:48], PS[:, 0, 32:48], ACT.Exp).then_inc(s["ed_ready"], 1)
                act.wait_ge(s["seg_mm"], i + 1)
                if i > 1:
                    act.wait_ge(s["y_mm"], i - 1)
                a.activation(ee2[i % 2][0:rows, :, 0:rows], seg_ps(PS, rows), ACT.Exp).then_inc(s["seg_exp"], 1)
                if i == 1:
                    for u in range(NT):
                        if u == 0:
                            act.wait_ge(s["z_ev"], 6)
                        a.activation(z[0:ROWS[u], u, :], z[0:ROWS[u], u, :], ACT.Silu).then_inc(s["z_silu"], 1)
                if i in (3, 5):
                    if i == 5:
                        mixed_out(0)
                    norm_mixed((i - 3) // 2)
            mixed_out(1)
            norm_mixed(2)
            mixed_out(2)
            step(a.activation(b_gu2[:, 0, :], b_gu[:, :], ACT.Copy))
            a.activation(b_dn2[:, 0, :], b_dn[:, :], ACT.Copy).then_inc(s["b_hi"], 1)
            for t in range(NT):
                act.wait_ge(s["x1_ready"], 2 * t + 2)
                step(a.activation(r6[0:ROWS[t], 3072:4096], x[0:ROWS[t], t, :], ACT.Square,
                                  accum_out=stat[0:ROWS[t], t:t + 1]))
                a.activation(stat[0:ROWS[t], 3 + t:4 + t], stat[0:ROWS[t], t:t + 1], ACT.Sqrt,
                             scale=1.0 / D, bias=stat[0:ROWS[t], 10:11]).then_inc(s["sqrt3"], 1)
            act.wait_ge(s["rexp"], 1)
            a.activation(pv[:, :, :], pv[:, :, :], ACT.Exp).then_inc(s["pv_ready"], 1)

            act.wait_ge(s["route_ready"], 1)
            for free in ("c_ready", "at_ev", "yy_ready"):
                act.sem_inc(s[free], 1)
            total = act.value_load(blocks[0:1, 0:1], min_val=NE, max_val=MAX_BLOCKS)
            act.wait_ge(s["xe_mm"], 1)
            a.activation(xe, bank(3), ACT.Copy).then_inc(s["xe_ev"], 1)
            with act.Fori(0, total) as b:
                act.wait_ge(s["ct_mm"], b + 1)
                act.wait_ge(s["comb_mm"], 6 * b + 6)
                a.activation(c01[0:64, 0, :], PS[0:64, 5, 0:TC], ACT.Copy)
                a.activation(c01[64:128, 1, :], PS[64:128, 5, 0:TC], ACT.Copy).then_inc(s["c_ready"], 1)
                act.wait_ge(s["g_ready"], b + 1)
                a.activation(sg, ug, ACT.Sigmoid, scale=ALPHA).then_inc(s["sig_ready"], 1)
                act.wait_ge(s["xe_mm"], b + 2)
                a.activation(xe, bank(3), ACT.Copy).then_inc(s["xe_ev"], 1)
                act.wait_ge(s["at_mm"], b + 1)
                a.activation(at.rearrange("p a b c -> p (a b c)"), bank(4), ACT.Copy).then_inc(s["at_ev"], 1)
                act.wait_ge(s["d_mm"], b + 1)
                a.activation(yy2[:, 0, :], bank(2), ACT.Copy).then_inc(s["yy_ready"], 1)
            for t in range(NT):
                act.wait_ge(s["o_ev"], 6 * total + 2 * t + 4)
                step(a.activation(r6[0:ROWS[t], 0:D], x[0:ROWS[t], t, :], ACT.Square,
                                  accum_out=stat[0:ROWS[t], t:t + 1]))
                a.activation(stat[0:ROWS[t], 3 + t:4 + t], stat[0:ROWS[t], t:t + 1], ACT.Sqrt,
                             scale=1.0 / D, bias=stat[0:ROWS[t], 10:11]).then_inc(s["sqrt4"], 1)

        @block.vector
        def _(dve):
            v = nc.vector
            vc = [0]

            def step(ins):
                vc[0] += 1
                ins.then_inc(s["vchain"], 1)
                dve.wait_ge(s["vchain"], vc[0])

            def states_out(n):
                for q in range(2):
                    dve.wait_ge(s["hst_mm"], 2 * n + q + 1)
                    if n and q == 0:
                        dve.wait_ge(s["sout_out"], 16)
                    v.tensor_copy(s_out[:, 4 * q:4 * q + 4, :], bank((7, 1)[q]).rearrange("p (k n) -> p k n", k=4))\
                        .then_inc(s["hst_ev"], 1)

            dve.wait_ge(s["small_in"], N_SMALL * 16)
            dve.wait_ge(s["consts"], 1)
            step(v.memset(stat[:, 10:11], EPS))
            v.tensor_copy(ext[:, 0:256], tab[:, 1:NREL])
            v.tensor_copy(ext[:, 256:383], bc(tab[:, 2 * CLIP:NREL], AH, 127)).then_inc(s["ext_out"], 1)
            dve.wait_ge(s["par_mm"], 1)
            v.tensor_copy(par[:, :], PS[:, 7, 0:88]).then_inc(s["par_ready"], 1)
            dve.wait_ge(s["ssq"], 1)
            v.tensor_scalar(stat[:, 3:6], stat[:, 3:6], 1.0 / D, EPS, ALU.mult, ALU.add).then_inc(s["rstd"], 1)
            dve.wait_ge(s["ssq"], 2)
            step(v.reciprocal(stat[:, 3:6], stat[:, 0:3]))
            for t in range(NT):
                rows = ROWS[t]
                v.tensor_scalar(x[0:rows, t, :], x[0:rows, t, :], stat[0:rows, 3 + t:4 + t], None, ALU.mult)\
                    .then_inc(s["xnorm"], 1)
            for i in range(6):
                t, h, rows = i // 2, i % 2, ROWS[i // 2]
                dve.wait_ge(s["hT_mm"], i + 1)
                v.tensor_tensor(hT[:, 4 * h:4 * h + 4, HCOL[t]:HCOL[t] + rows],
                                PS[:, i, :].rearrange("p (k n) -> p k n", k=4)[:, :, 0:rows],
                                bc(gmix[:, 4 * h:4 * h + 4].unsqueeze(2), 128, 4, rows), ALU.mult)\
                    .then_inc(s["hT_ready"], 1)
            dve.wait_ge(s["ck_mm"], 1)
            v.tensor_copy(ckT[:, :, :], bank(7).rearrange("p (k n) -> p k n", k=4)).then_inc(s["ck_ready"], 1)
            dve.wait_ge(s["hist_mm"], 1)
            step(v.tensor_copy(prevT[:, :, :], PS[:, 6, 0:36].rearrange("p (k n) -> p k n", n=3)))
            for c in range(CT):
                dve.wait_ge(s["proj_ev"], c + 1)
                step(v.tensor_copy(pad[:, c, 259:262], prevT[:, c, :]))
                step(v.tensor_scalar(conv[:, c, :], pad[:, c, 0:HC], cw[:, c, 0:1], cb[:, c:c + 1], ALU.mult, ALU.add))
                for j in range(1, TAPS):
                    ins = v.scalar_tensor_tensor(conv[:, c, :], pad[:, c, j:j + HC], cw[:, c, j:j + 1],
                                                 conv[:, c, :], ALU.mult, ALU.add)
                    if j < TAPS - 1:
                        step(ins)
                ins.then_inc(s["conv_done"], 1)
            v.tensor_copy(cst[:, :, 0:3], pad[:, :, 256:259])
            v.tensor_copy(cst[:, :, 3:6], pad[:, :, HC:HC + 3]).then_inc(s["cst_ready"], 1)
            dve.wait_ge(s["cst_ready"], 1)
            dve.wait_ge(s["t2_mm"], 1)
            step(v.memset(dta[:, 2, :], 0.0))
            for t in range(NT):
                step(v.tensor_tensor(dA[0:ROWS[t], t, :], PS[0:ROWS[t], 4, 16 * t:16 * t + 16],
                                     dtb[0:ROWS[t], :], ALU.add))
            step(v.memset(dA[64:128, 2, :], 0.0))
            step(v.tensor_scalar(dt[:, :, :], dA[:, :, :], -1.0, None, ALU.mult))
            v.tensor_tensor(dta[:, :, :], dA[:, :, :], dt[:, :, :], ALU.max).then_inc(s["dtc_ready"], 1)
            for t in range(NT):
                rows = ROWS[t]
                dve.wait_ge(s["t2_mm"], 3 * t + 2)
                v.tensor_copy(xs[0:rows, t, 0:512], PS[0:rows, 5, :]).then_inc(s["t2_dve"], 1)
                dve.wait_ge(s["t2_mm"], 3 * t + 3)
                v.tensor_copy(xs[0:rows, t, 512:1024], PS[0:rows, 6, :]).then_inc(s["t2_dve"], 1)
                dve.wait_ge(s["t2_mm"], 3 * t + 4)
                v.tensor_copy(bt[0:rows, t, :], PS[0:rows, 4, 64:320]).then_inc(s["t2_dve"], 1)
            for i in range(3):
                dve.wait_ge(s["cst_mm"], i + 1)
                v.tensor_copy(cso[0:6, 512 * i:512 * i + 512], PS[0:6, i, :]).then_inc(s["cso_ready"], 1)
            dve.wait_ge(s["ln_done"], 1)
            step(v.tensor_scalar(dA[:, :, :], dA[:, :, :], 0.0, None, ALU.max))
            step(v.tensor_tensor(dt[:, :, :], dA[:, :, :], dtt[:, :, :], ALU.add))
            step(v.scalar_tensor_tensor(dA[:, :, :], dt[:, :, :], -1.0,
                                        bc(alog[:, :].unsqueeze(1), 128, NT, HEADS), ALU.mult, ALU.mult))
            dve.wait_ge(s["bias_in"], 64)
            step(v.memset(bias[0:64, :, 0:64], NEG))
            dve.wait_ge(s["cso_out"], 32)
            for i in range(7):
                if i < 6:
                    t, hg, rows = i // 2, i % 2, ROWS[i // 2]
                    nk, b0 = ((128, 128), (256, 0), (PAST + SS, 0))[t]
                    dve.wait_ge(s["qk_mm"], i + 1)
                    if i:
                        dve.wait_ge(s["pT_mm"], i)
                    step(v.scalar_tensor_tensor(
                        sc[0:rows, :, 0:nk],
                        PS[0:rows, 2 * (i % 2):2 * (i % 2) + 2, :].rearrange("p b (h n) -> p (b h) n", h=2)[:, :, 0:nk],
                        float(AD) ** -0.5, backwards(bias[0:rows, 4 * hg:4 * hg + 4, :], 255 - b0, nk), ALU.mult, ALU.add))
                    if i:
                        if i > 1:
                            dve.wait_ge(s["o_ready"], i - 1)
                        step(v.reciprocal(rs[:, :], sm[:, :]))
                    v.tensor_reduce(mx[0:rows, :], sc[0:rows, :, 0:nk], axis=X, op=ALU.max, negate=True)\
                        .then_inc(s["mx_ready"], 1)
                if i:
                    tp, hp, rp = (i - 1) // 2, (i - 1) % 2, ROWS[(i - 1) // 2]
                    if i == 6:
                        dve.wait_ge(s["o_ready"], i - 1)
                        step(v.reciprocal(rs[:, :], sm[:, :]))
                    dve.wait_ge(s["pv_mm"], i)
                    v.tensor_tensor(ot[0:rp, tp, 256 * hp:256 * hp + 256].rearrange("p (h b d) -> p b h d", b=2, d=AD),
                                    PS[0:rp, 6, 0:256].rearrange("p (b h d) -> p b h d", b=2, d=AD),
                                    bc(rs[0:rp, :].rearrange("p (b h) -> p b h", b=2).unsqueeze(3), rp, 2, 2, AD),
                                    ALU.mult).then_inc(s["o_ready"], 1)
                if i < 6:
                    nt = 8 if nk > 128 else 4
                    dve.wait_ge(s["pT_mm"], i + 1)
                    v.tensor_copy(pT[:, 0:nt, 0:rows],
                                  PS[:, 4:6, :].rearrange("p b (h n) -> p (b h) n", h=4)[:, 0:nt, 0:rows])\
                        .then_inc(s["pT_ready"], 1)
            def heads(b, rows):
                return PS[0:rows, b, :].rearrange("p (h d) -> p h d", d=P_HEAD)

            def xh(i):
                return xs[0:ROWS[i // 2], i // 2, 512 * (i % 2):512 * (i % 2) + 512].rearrange("p (h d) -> p h d", d=P_HEAD)

            def segments(i):
                t, gg, rows = i // 2, i % 2, ROWS[i // 2]
                v.tensor_tensor(dau[0:rows, :, 0:rows], bc(dA[0:rows, t, 8 * gg:8 * gg + 8].unsqueeze(2), rows, 8, rows),
                                bc(upper[0:rows, 0:rows].unsqueeze(1), rows, 8, rows), ALU.mult)\
                    .then_inc(s["dau_ready"], 1)

            def operands(i):
                t, gg, rows = i // 2, i % 2, ROWS[i // 2]
                hs = slice(8 * gg, 8 * gg + 8)
                xdt, xw, ee = xdt2[i % 2], xw2[i % 2], ee2[i % 2]
                if gg == 0:
                    dve.wait_ge(s["ed_ready"], t + 1)
                    ins = v.tensor_tensor(gm[0:rows, :, 0:rows],
                                          PS[0:rows, 0, 64:320].rearrange("p (g n) -> p g n", g=2)[:, :, 0:rows],
                                          bc(upper[0:rows, 0:rows].unsqueeze(1), rows, 2, rows), ALU.mult)
                    ins.then_inc(s["gm_ready"], 1)
                    dve.wait_ge(s["gm_ready"], t + 1)
                if i == 1:
                    dve.wait_ge(s["ktv_out"], 6 * 16)
                step(v.tensor_tensor(xdt[0:rows], xh(i), bc(dt[0:rows, t, hs].unsqueeze(2), rows, 8, P_HEAD), ALU.mult))
                v.tensor_tensor(xw[0:rows], xdt[0:rows],
                                bc(edec[0:rows, t, 16 + 8 * gg:24 + 8 * gg].unsqueeze(2), rows, 8, P_HEAD), ALU.mult)\
                    .then_inc(s["xw_ready"], 1)
                if i < 5:
                    dve.wait_ge(s["seg_mm"], i + 1)
                    segments(i + 1)
                dve.wait_ge(s["seg_exp"], i + 1)
                v.tensor_tensor(ee[0:rows, :, 0:rows], ee[0:rows, :, 0:rows],
                                bc(gm[0:rows, gg, 0:rows].unsqueeze(1), rows, 8, rows), ALU.mult)\
                    .then_inc(s["m_ready"], 1)

            dve.wait_ge(s["o_ready"], 6)
            dve.wait_ge(s["pT_mm"], 6)
            segments(0)
            operands(0)
            for i in range(6):
                t, gg, rows = i // 2, i % 2, ROWS[i // 2]
                hs = slice(8 * gg, 8 * gg + 8)
                if i < 5:
                    operands(i + 1)
                step(v.tensor_tensor(acc[0:rows], xh(i), bc(dsk[0:rows, hs].unsqueeze(2), rows, 8, P_HEAD), ALU.mult))
                dve.wait_ge(s["y_mm"], i + 1)
                zh = z[0:rows, t, 512 * gg:512 * gg + 512].rearrange("p (h d) -> p h d", d=P_HEAD)
                hh = (hst, hst_s)[t // 2][:, 512 * gg:512 * gg + 512].rearrange("p (h d) -> p h d", d=P_HEAD)
                step(v.tensor_tensor(acc[0:rows], acc[0:rows], heads(4, rows), ALU.add))
                if t:
                    step(v.tensor_tensor(yo[0:rows], heads(5, rows),
                                         bc(edec[0:rows, t, 8 * gg:8 * gg + 8].unsqueeze(2), rows, 8, P_HEAD), ALU.mult))
                    step(v.tensor_tensor(hh, hh, bc(edec[:, t, 32 + 8 * gg:40 + 8 * gg].unsqueeze(2), 128, 8, P_HEAD), ALU.mult))
                    v.tensor_tensor(hh, hh, heads(6, 128), ALU.add).then_inc(s["yb_free"], 1)
                    step(v.tensor_tensor(acc[0:rows], acc[0:rows], yo[0:rows], ALU.add))
                else:
                    v.tensor_copy(hh, heads(6, 128)).then_inc(s["yb_free"], 1)
                if i == 0:
                    dve.wait_ge(s["z_silu"], NT)
                v.tensor_tensor(zh, acc[0:rows], zh, ALU.mult).then_inc(s["y_ev"], 1)
                if i == 1:
                    for q in range(2):
                        dve.wait_ge(s["sraw_mm"], q + 1)
                        v.tensor_copy(hst_s[:, 512 * q:512 * q + 512], bank((7, 1)[q])).then_inc(s["sraw_ev"], 1)
                if i == 4:
                    states_out(0)
                if i in (2, 4, 5):
                    u = (i - 1) // 2 if i < 5 else 2
                    dve.wait_ge(s["sqrt2"], u + 1)
                    ss = stat[0:ROWS[u], 12 + 3 * u:15 + 3 * u]
                    v.reciprocal(ss, ss).then_inc(s["rec2"], 1)
            states_out(1)
            step(v.memset(xn[:, 2, :], 0.0))
            step(v.memset(lg[:, :, :], 0.0))
            for t in range(NT):
                rows = ROWS[t]
                dve.wait_ge(xres_in[t], 16)
                for h in range(2):
                    i = 2 * t + h
                    dve.wait_ge(s["out_mm"], i + 1)
                    parts = 1 if t < 2 else 2
                    for q in range(parts):
                        n = 512 // parts
                        xx = x[0:rows, t, 512 * h + n * q:512 * h + n * q + n]
                        ins = v.tensor_tensor(xx, xx, PS[64 * q:64 * q + rows, out_bank(i), 0:n], ALU.add)
                    ins.then_inc(s["x1_ready"], 1)
                if t == 1:
                    dve.wait_ge(s["b_hi"], 1)
                    step(v.tensor_tensor(b_gu2[:, 1, :], b_gu[:, :], b_gu2[:, 0, :].bitcast(f32), ALU.subtract))
                    step(v.tensor_tensor(b_dn2[:, 1, :], b_dn[:, :], b_dn2[:, 0, :].bitcast(f32), ALU.subtract))
                    step(v.memset(c01[:, :, :].bitcast(f32), 0.0))
                    step(v.memset(gprev[:, :], 0.0))
                    step(v.memset(yy2[:, :, :].bitcast(f32), 0.0))
                dve.wait_ge(s["sqrt3"], t + 1)
                step(v.reciprocal(stat[0:rows, 6 + t:7 + t], stat[0:rows, 3 + t:4 + t]))
                v.tensor_scalar(xn[0:rows, t, :], x[0:rows, t, :], stat[0:rows, 6 + t:7 + t], None, ALU.mult)\
                    .then_inc(s["xn_ready"], 1)
                for h in range(2):
                    i = 2 * t + h
                    dve.wait_ge(s["hf_mm"], i + 1)
                    v.tensor_tensor(hfT[:, 4 * h:4 * h + 4, TCOL[t]:TCOL[t] + rows],
                                    PS[:, (6, 0)[h], :].rearrange("p (k n) -> p k n", k=4)[:, :, 0:rows],
                                    bc(gffn[:, 4 * h:4 * h + 4].unsqueeze(2), 128, 4, rows), ALU.mult)\
                        .then_inc(s["hf_ready"], 1)
                dve.wait_ge(s["lgt_mm"], t + 1)
                step(v.tensor_tensor(lg[0:rows, t, :], PS[0:rows, 1, 32 * t:32 * t + 32], brt[0:rows, :], ALU.add))
                step(v.max(m8[:, t, :], lg[:, t, :]))
                step(v.max_index(i8[:, t, :], m8[:, t, :], lg[:, t, :]))
            v.tensor_tensor(pv[:, :, :], m8[:, :, 0:4], bc(m8[:, :, 0:1], 128, NT, 4), ALU.subtract)\
                .then_inc(s["rexp"], 1)
            step(v.tensor_copy(ix[:, :, :], i8[:, :, :]))
            step(v.tensor_tensor(eq[:, :, :, :], bc(iota[:, 0:NE].unsqueeze(1).unsqueeze(1), 128, NT, TOPK, NE),
                                 bc(ix[:, :, 0:TOPK].unsqueeze(3), 128, NT, TOPK, NE), ALU.is_equal))
            dve.wait_ge(s["pv_ready"], 1)
            step(v.tensor_reduce(chosen[:, :, :], eq[:, :, :, :].rearrange("p t k e -> p t e k"), axis=X, op=ALU.add))
            v.memset(chosen[64:128, 2, :], 0.0).then_inc(s["rexp"], 1)
            step(v.tensor_reduce(ps4[:, :], pv[:, :, :], axis=X, op=ALU.add))
            step(v.reciprocal(ps4[:, :], ps4[:, :]))
            step(v.tensor_tensor(pv[:, :, :], pv[:, :, :], bc(ps4[:, :].unsqueeze(2), 128, NT, 4), ALU.mult))
            step(v.tensor_tensor(eq[:, :, :, :], eq[:, :, :, :], bc(pv[:, :, :].unsqueeze(3), 128, NT, TOPK, NE), ALU.mult))
            step(v.tensor_reduce(pg[:, :, NT:2 * NT].rearrange("p e t -> p t e"),
                                 eq[:, :, :, :].rearrange("p t k e -> p t e k"), axis=X, op=ALU.add))
            dve.wait_ge(s["rexp"], 2)
            dve.wait_ge(s["pos_mm"], 1)
            step(v.scalar_tensor_tensor(one[:, :, :], PS[:, 6, 0:96].rearrange("p (t e) -> p t e", e=NE), 1.0,
                                        chosen[:, :, :], ALU.add, ALU.mult))
            step(v.tensor_scalar(pg[:, :, 0:NT].rearrange("p e t -> p t e"), one[:, :, :], -1.0, None, ALU.add))
            count, nb, upto, t3 = PS[:, 6, 96:128], nbk[:, 0, :], nbk[:, 1, :], nbk[:, 2, :]
            step(v.memset(nbk[:, 3, :], 0.0))
            step(v.tensor_scalar(nb, count, float(CAP), 1.0, ALU.is_gt, ALU.add))
            for m in range(2, TC // CAP):
                step(v.scalar_tensor_tensor(nb, count, float(CAP * m), nb, ALU.is_gt, ALU.add))
            step(v.tensor_tensor_scan(upto, nb, nbk[:, 3, :], 0.0, ALU.add, ALU.add))
            step(v.tensor_scalar(t3, upto, pidx[:, 0:1], None, ALU.is_le))
            step(v.tensor_reduce(bej[:, 0:1], t3, axis=X, op=ALU.add))
            step(v.tensor_tensor(t3, t3, nb, ALU.mult))
            step(v.tensor_reduce(bej[:, 1:2], t3, axis=X, op=ALU.add))
            step(v.tensor_scalar(bej[:, 0:1], bej[:, 0:1], float(NE - 1), None, ALU.min))
            v.tensor_tensor(bej[:, 1:2], pidx[:, :], bej[:, 1:2], ALU.subtract).then_inc(s["bej_ready"], 1)
            step(v.tensor_tensor(t3[0:1], upto[0:1], nb[0:1], ALU.subtract))
            step(v.tensor_copy(before[:, :], t3[0:1]))
            step(v.tensor_copy(blocks[:, :], upto[0:1, NE - 1:NE]))
            dve.wait_ge(s["bej_mm"], 1)
            step(v.tensor_copy(expert_of[:, :], PS[0:1, 7, 0:128]))
            v.tensor_scalar(place_of[:, :], PS[0:1, 7, 128:256], 0.0, None, ALU.max).then_inc(s["route_ready"], 1)
            dve.wait_ge(s["route_ready"], 1)
            dve.sem_inc(s["o_ev"], 2)
            for free in ("gu_ev", "yyl_ready", "gates_held"):
                dve.sem_inc(s[free], 1)
            total = dve.value_load(blocks[0:1, 0:1], min_val=NE, max_val=MAX_BLOCKS)

            def one_hots(b, e, j):
                v.tensor_copy(pcur[:, :], pg[:, bass.ds(e, 1), :].rearrange("p a n -> p (a n)")).then_inc(s["pcur_ready"], 1)
                dve.wait_ge(s["pcur_ready"], b + 1)
                for t in range(NT):
                    v.tensor_scalar(pm[:, t, :].rearrange("p (a n) -> p a n", a=2),
                                    bc(iota[:, bass.ds(j * CAP, CAP)].unsqueeze(1), 128, 2, CAP),
                                    pcur[:, t:t + 1], None, ALU.is_equal).then_inc(s["p_ready"], 1)

            def selector(dst, e, n, name):
                v.tensor_copy(dst, bc(ident[:, 0:NE * n].rearrange("p (c e) -> p c e", e=NE)[:, :, bass.ds(e, 1)],
                                      128, n, CAP)).then_inc(s[name], 1)

            def gathered(b):
                dve.wait_ge(s["xt_mm"], b + 1)
                v.tensor_tensor(xt, bank(3).rearrange("p (c h n) -> p c h n", c=4, h=2),
                                bc(gffn[:, :].rearrange("p (h c) -> p c h", h=2).unsqueeze(3), 128, 4, 2, CAP),
                                ALU.mult).then_inc(s["xt_ev"], 1)

            def accumulate(n):
                for i in range(6):
                    t, h, rows = i // 2, i % 2, ROWS[i // 2]
                    dve.wait_ge(s["comb_mm"], n + i + 1)
                    xx = x[0:rows, t, 512 * h:512 * h + 512]
                    v.scalar_tensor_tensor(xx, PS[0:rows, 6 + h, :], gprev[0:rows, t:t + 1], xx, ALU.mult, ALU.add)\
                        .then_inc(s["o_ev"], 1)

            one_hots(0, 0, 0)
            selector(sel[:, :, :], 0, 4, "sel_ready")
            gathered(0)
            with dve.Fori(0, total) as b:
                e = dve.value_load(expert_of[0:1, bass.ds(b, 1)], min_val=0, max_val=NE - 1)
                e_next = dve.value_load(expert_of[0:1, bass.ds(b + 1, 1)], min_val=0, max_val=NE - 1)
                j_next = dve.value_load(place_of[0:1, bass.ds(b + 1, 1)], min_val=0, max_val=TC // CAP - 1)
                selector(sel_dn[:, :, :], e, 2, "seld_ready")
                dve.wait_ge(s["gates_held"], b + 1)
                accumulate(6 * b)
                dve.wait_ge(s["o_ev"], 6 * b + 8)
                v.tensor_copy(gprev[:, :], pcur[:, NT:2 * NT]).then_inc(s["gates_held"], 1)
                dve.wait_ge(s["gates_held"], b + 2)
                dve.wait_ge(s["ct_mm"], b + 1)
                one_hots(b + 1, e_next, j_next)
                dve.wait_ge(s["gs_used"], b + 1)
                selector(sel[:, :, :], e_next, 4, "sel_ready")
                dve.wait_ge(s["gu_mm"], b + 1)
                v.tensor_scalar(ug, bank(0), LIMIT, None, ALU.min).then_inc(s["g_ready"], 1)
                v.tensor_scalar(uu, bank(1), LIMIT, -LIMIT, ALU.min, ALU.max).then_inc(s["gu_ev"], 1)
                dve.wait_ge(s["sig_ready"], b + 1)
                v.tensor_tensor(ug, ug, sg, ALU.mult).then_inc(s["act_ready"], 1)
                dve.wait_ge(s["act_ready"], 2 * b + 1)
                v.scalar_tensor_tensor(ac, uu, 1.0, ug, ALU.add, ALU.mult).then_inc(s["act_ready"], 1)
                gathered(b + 1)
                dve.wait_ge(s["yy_ready"], b + 2)
                v.tensor_tensor(yy2[:, 1, :], bank(2), yy2[:, 0, :].bitcast(f32), ALU.subtract)\
                    .then_inc(s["yyl_ready"], 1)
            dve.wait_ge(s["gates_held"], total + 1)
            accumulate(6 * total)
            dve.wait_ge(s["gfin_in"], 16)
            for t in range(NT):
                rows = ROWS[t]
                dve.wait_ge(s["sqrt4"], t + 1)
                step(v.reciprocal(stat[0:rows, 6 + t:7 + t], stat[0:rows, 3 + t:4 + t]))
                v.scalar_tensor_tensor(xn[0:rows, t, :], x[0:rows, t, :], stat[0:rows, 6 + t:7 + t],
                                       gfin[0:rows], ALU.mult, ALU.mult).then_inc(s["fin_ready"], 1)

        @block.tensor
        def _(pe):
            mm = nc.tensor.matmul

            def tr(out, in_):
                k = in_.shape[0]
                return nc.tensor.transpose(out, in_, ident[0:k, 0:k])

            pe.wait_ge(s["consts"], 1)
            pe.wait_ge(s["small_in"], N_SMALL * 16)
            tr(PS[:, 7, 0:88], praw[:, :]).then_inc(s["par_mm"], 1)
            for i in range(6):
                t, h, rows = i // 2, i % 2, ROWS[i // 2]
                pe.wait_ge(s["xnorm"], t + 1)
                for q in range(4):
                    k = 4 * h + q
                    last = tr(PS[:, i, 128 * q:128 * q + rows], x[0:rows, t, 128 * k:128 * k + 128])
                last.then_inc(s["hT_mm"], 1)
            pe.wait_ge(s["par_ready"], 1)
            for q in range(4):
                last = tr(PS[:, 7, 128 * q:128 * q + 128], ck[:, 128 * q:128 * q + 128])
            last.then_inc(s["ck_mm"], 1)
            pe.wait_ge(s["cvhist_in"], 16)
            for c in range(CT):
                last = tr(PS[:, 6, 3 * c:3 * c + 3], hraw[0:3, 128 * c:128 * c + 128])
            last.then_inc(s["hist_mm"], 1)
            pe.wait_ge(s["hT_ready"], 6)
            n = [0]

            def group(emit):
                if n[0] >= 4:
                    pe.wait_ge(s["proj_ev"], n[0] - 3)
                last = emit(n[0] % 4)
                last.then_inc(s["proj_mm"], 1)
                n[0] += 1

            def chunk(i):
                pe.wait_ge(w_full[slot_of(i)], front_arrival(i))
                return ring[:, slot_of(i), :].rearrange("p (k n) -> p k n", k=KD)

            def features(w, m):
                def emit(b):
                    for k in range(KD):
                        last = mm(PS[:, b, 0:HC], w[:, k, 128 * m:128 * m + 128], hT[:, k, :],
                                  start=(k == 0), stop=(k == KD - 1))
                    return last
                return emit

            def rows_by(b, t, lhs, rhs, first, end):
                if t < 2:
                    return mm(PS[:, b, :], lhs, rhs, start=first, stop=end)
                for q in range(2):
                    last = mm(PS[64 * q:64 * q + 64, b, 0:256], lhs, rhs[:, 256 * q:256 * q + 256],
                              start=first, stop=end)
                return last

            def tokens(w, t):
                def emit(b):
                    for k in range(KD):
                        last = rows_by(b, t, hT[:, k, HCOL[t]:HCOL[t] + ROWS[t]], w[:, k, :], k == 0, k == KD - 1)
                    return last
                return emit

            def dt_rows(b):
                for k in range(KD):
                    last = mm(PS[0:HEADS, b, 0:HC], wdt[:, k, :], hT[:, k, :], start=(k == 0), stop=(k == KD - 1))
                return last

            for i in range(5):
                w = chunk(i)
                for m in range(4):
                    group(features(w, m))
            group(dt_rows)
            w = chunk(5)
            for t in range(NT):
                group(tokens(w, t))
            pe.wait_ge(s["proj_ev"], 21)
            for t in range(NT):
                last = tr(PS[0:ROWS[t], 4, 16 * t:16 * t + 16], dtT[:, HCOL[t]:HCOL[t] + ROWS[t]])
            last.then_inc(s["t2_mm"], 1)
            pe.wait_ge(s["silu_done"], 3)
            pe.wait_ge(s["dtc_ready"], 1)
            for t in range(NT):
                rows, hc = ROWS[t], slice(HCOL[t], HCOL[t] + ROWS[t])
                for h in range(2):
                    if t:
                        pe.wait_ge(s["t2_dve"], 3 * t - 2 + h)
                    for q in range(4):
                        last = tr(PS[0:rows, 5 + h, 128 * q:128 * q + 128], conv[:, 4 * h + q, hc])
                    last.then_inc(s["t2_mm"], 1)
                if t:
                    pe.wait_ge(s["t2_dve"], 3 * t)
                    pe.wait_ge(s["t2_act"], t)
                for q in range(2):
                    tr(PS[0:rows, 4, 64 + 128 * q:64 + 128 * q + 128], conv[:, XT + q, hc])
                for q in range(4):
                    last = tr(PS[0:rows, 7, 128 * q:128 * q + 128], qk[:, 4 + q, hc])
                last.then_inc(s["t2_mm"], 1)
            pe.wait_ge(s["cst_ready"], 1)
            pe.wait_ge(s["proj_ev"], n[0])
            for i in range(3):
                for q in range(4):
                    last = tr(PS[0:6, i, 128 * q:128 * q + 128], cst[:, 4 * i + q, :])
                last.then_inc(s["cst_mm"], 1)
            pe.wait_ge(s["cso_ready"], 3)
            pe.wait_ge(s["t2_dve"], 9)
            pe.wait_ge(s["t2_act"], 3)

            def scores(i):
                t, hg, rows = i // 2, i % 2, ROWS[i // 2]
                if i >= 2:
                    pe.wait_ge(s["mx_ready"], i - 1)
                for h in range(4):
                    head = head_of(hg, h)
                    par = slice(64 * (head % 2), 64 * (head % 2) + 64)
                    q_ = qk[par, head // 2, HCOL[t]:HCOL[t] + rows]
                    o = PS[0:rows, 2 * (i % 2) + h // 2, :]
                    at0 = 256 * (h % 2)
                    if t < 2:
                        nk = 128 * (t + 1)
                        last = mm(o[:, at0:at0 + nk], q_, qk[par, 4 + head // 2, 0:nk], start=True, stop=True)
                    else:
                        mm(o[:, at0:at0 + PAST], q_, ckT[par, head // 2, :], start=True, stop=True)
                        last = mm(o[:, at0 + PAST:at0 + PAST + SS], q_,
                                  qk[par, 4 + head // 2, HCOL[2]:HCOL[2] + SS], start=True, stop=True)
                last.then_inc(s["qk_mm"], 1)

            def z_part(i, part):
                h, t = i // NT, i % NT
                if part == 0:
                    w = chunk(6 + h)
                    if i:
                        pe.wait_ge(s["z_ev"], i)
                w = ring[:, slot_of(6 + h), :].rearrange("p (k n) -> p k n", k=KD)
                for k in range(KD // 2 * part, KD // 2 * (part + 1)):
                    last = rows_by(7, t, hT[:, k, HCOL[t]:HCOL[t] + ROWS[t]], w[:, k, :], k == 0, k == KD - 1)
                if part:
                    last.then_inc(s["z_mm"], 1)

            scores(0)
            for i in range(6):
                t, hg, rows = i // 2, i % 2, ROWS[i // 2]
                if i < 5:
                    scores(i + 1)
                z_part(i, 0)
                keys = ([128], [128, 128], [PAST, SS])[t]
                pe.wait_ge(s["exp_ready"], i + 1)
                if i:
                    pe.wait_ge(s["pT_ready"], i)
                for h in range(4):
                    for kk, nk in enumerate(keys):
                        c = len(keys) * h + kk
                        last = tr(PS[0:nk, 4 + c // 4, 128 * (c % 4):128 * (c % 4) + rows],
                                  sc[0:rows, h, 128 * kk:128 * kk + nk])
                last.then_inc(s["pT_mm"], 1)
                z_part(i, 1)
                pe.wait_ge(s["pT_ready"], i + 1)
                if i:
                    pe.wait_ge(s["o_ready"], i)
                for h in range(4):
                    head = head_of(hg, h)
                    for kk, nk in enumerate(keys):
                        c = len(keys) * h + kk
                        if t == 2:
                            vals = (cv[:, :], vt[0:SS, 2, :])[kk]
                        else:
                            vals = vt[:, kk, :]
                        last = mm(PS[0:rows, 6, 64 * h:64 * h + 64], pT[0:nk, c, 0:rows],
                                  vals[:, 64 * head:64 * head + 64], start=(kk == 0), stop=(kk == len(keys) - 1))
                last.then_inc(s["pv_mm"], 1)
            def sums(t):
                rows, hc = ROWS[t], slice(HCOL[t], HCOL[t] + ROWS[t])
                if t:
                    pe.wait_ge(s["ed_ready"], t)
                    pe.wait_ge(s["gm_ready"], t)
                mm(PS[0:rows, 0, 0:16], upper[0:rows, 0:rows], dA[0:rows, t, :], start=True, stop=True)
                mm(PS[0:rows, 0, 16:32], lower[0:rows, 0:rows], dA[0:rows, t, :], start=True, stop=True)
                mm(PS[:, 0, 32:48], ones[0:rows, :], dA[0:rows, t, :], start=True, stop=True)
                for q in range(2):
                    last = mm(PS[0:rows, 0, 64 + 128 * q:64 + 128 * q + rows], conv[:, XT + q, hc],
                              conv[:, XT + 2 + q, hc], start=True, stop=True)
                last.then_inc(s["gt_mm"], 1)

            def segment_sums(i):
                rows = ROWS[i // 2]
                pe.wait_ge(s["dau_ready"], i + 1)
                if i % 2 == 0:
                    sums(i // 2)
                if i:
                    pe.wait_ge(s["seg_exp"], i)
                for q in range(2):
                    last = mm(PS[0:rows, 2 + q, 0:4 * rows], lower[0:rows, 0:rows], dau[0:rows, 4 * q:4 * q + 4, 0:rows],
                              start=True, stop=True)
                last.then_inc(s["seg_mm"], 1)

            def turn_states(src, name):
                for q in range(2):
                    for c in range(4):
                        last = tr(PS[:, (7, 1)[q], 128 * c:128 * c + 128], src(4 * q + c))
                    last.then_inc(s[name], 1)

            def turn_mixed(t):
                rows = ROWS[t]
                for q in range(3):
                    i = 3 * t + q
                    pe.wait_ge(s["mixn"], i + 1)
                    if q == 2:
                        pe.wait_ge(s["mixT_ready"], i - 1)
                    for c in range(4):
                        src = z[0:rows, t, 512 * q + 128 * c:512 * q + 128 * c + 128] if q < 2 else \
                            ot[0:rows, t, 128 * c:128 * c + 128]
                        last = tr(PS[:, mix_bank(i), 128 * c:128 * c + rows], src)
                    last.then_inc(s["mixT_mm"], 1)

            segment_sums(0)
            for i in range(6):
                t, gg, rows = i // 2, i % 2, ROWS[i // 2]
                hc = slice(HCOL[t], HCOL[t] + rows)
                state = (hst, hst_s)[t // 2]
                if i < 5:
                    segment_sums(i + 1)
                if i == 1:
                    pe.wait_ge(s["sraw_in"], 16)
                    pe.wait_ge(s["z_ev"], 6)
                    turn_states(lambda c: s_raw[:, c, :], "sraw_mm")
                if i == 4:
                    pe.wait_ge(s["sraw_ev"], 2)
                    pe.wait_ge(s["yb_free"], 4)
                    turn_states(lambda c: hst[:, 128 * c:128 * c + 128], "hst_mm")
                pe.wait_ge(s["xw_ready"], i + 1)
                pe.wait_ge(s["m_ready"], i + 1)
                if i:
                    pe.wait_ge(s["yb_free"], i)
                xdt, xw, ee = xdt2[i % 2], xw2[i % 2], ee2[i % 2]
                for h in range(8):
                    mm(PS[0:rows, 4, 64 * h:64 * h + 64], ee[0:rows, h, 0:rows], xdt[0:rows, h, :], start=True, stop=True)
                if t:
                    mm(PS[0:rows, 5, :], conv[:, XT + 2 + gg, hc], state[:, 512 * gg:512 * gg + 512], start=True, stop=True)
                mm(PS[:, 6, :], bt[0:rows, t, 128 * gg:128 * gg + 128], xw[0:rows].rearrange("p h d -> p (h d)"),
                   start=True, stop=True).then_inc(s["y_mm"], 1)
            def project(t, h):
                rows = ROWS[t]
                i = 2 * t + h
                pe.wait_ge(s["mixT_ready"], 3 * t + 3)
                if i == 0:
                    for j in range(N_OUT):
                        pe.wait_ge(w_full[slot_of(N_IN + j)], front_arrival(N_IN + j))
                if i >= 4:
                    pe.wait_ge(s["x1_ready"], i - 3)
                for k in range(MT):
                    w = ring[:, slot_of(N_IN + k // 4), :].rearrange("p (k n) -> p k n", k=4)
                    last = rows_by(out_bank(i), t, mixT[:, k, TCOL[t]:TCOL[t] + rows],
                                   w[:, k % 4, 512 * h:512 * h + 512], k == 0, k == MT - 1)
                last.then_inc(s["out_mm"], 1)

            def logits(t):
                rows, tc = ROWS[t], slice(TCOL[t], TCOL[t] + ROWS[t])
                pe.wait_ge(s["xn_ready"], t + 1)
                for h in range(2):
                    for c in range(4):
                        last = tr(PS[:, (6, 0)[h], 128 * c:128 * c + rows],
                                  xn[0:rows, t, 512 * h + 128 * c:512 * h + 128 * c + 128])
                    last.then_inc(s["hf_mm"], 1)
                pe.wait_ge(s["hf_ready"], 2 * t + 2)
                for k in range(KD):
                    last = mm(PS[0:rows, 1, 32 * t:32 * t + 32], hfT[:, k, tc], wr[:, k, :],
                              start=(k == 0), stop=(k == KD - 1))
                last.then_inc(s["lgt_mm"], 1)

            pe.wait_ge(s["hst_ev"], 2)
            turn_mixed(0)
            pe.wait_ge(s["seg_exp"], 6)
            project(0, 0)
            pe.wait_ge(s["mixT_ready"], 3)
            turn_mixed(1)
            project(0, 1)
            pe.wait_ge(s["mixT_ready"], 6)
            pe.wait_ge(s["y_ev"], 6)
            turn_states(lambda c: hst_s[:, 128 * c:128 * c + 128], "hst_mm")
            project(1, 0)
            pe.wait_ge(s["hst_ev"], 4)
            turn_mixed(2)
            project(1, 1)
            pe.wait_ge(s["mixT_ready"], 9)
            logits(0)
            project(2, 0)
            logits(1)
            project(2, 1)
            logits(2)
            pe.wait_ge(s["rexp"], 2)
            for t in range(NT + 1):
                cols = slice(32 * t, 32 * t + 32)
                for u in range(min(t, NT - 1) + 1):
                    k = ROWS[u]
                    lhs = strict[0:k, :] if u == t else ones[0:k, :]
                    last = mm(PS[:, 6, cols], lhs, chosen[0:k, u, :], start=(u == 0), stop=(u == min(t, NT - 1)))
            last.then_inc(s["pos_mm"], 1)

            pe.wait_ge(s["bej_ready"], 1)
            for c in range(2):
                last = tr(PS[0:1, 7, 128 * c:128 * c + 128], bej[:, c:c + 1])
            last.then_inc(s["bej_mm"], 1)

            def gather(b):
                pe.wait_ge(s["p_ready"], 3 * b + 3)
                for t in range(NT):
                    for h in range(2):
                        last = mm(PS[64 * h:64 * h + 64, 3, :], pm[:, t, 64 * h:64 * h + 64],
                                  xn[:, t, 512 * h:512 * h + 512], start=(t == 0), stop=(t == NT - 1))
                last.then_inc(s["xe_mm"], 1)
                pe.wait_ge(s["c_ready"], b + 1)
                for t in range(NT):
                    last = tr(PS[:, 5, 128 * t:128 * t + 128], pm[:, t, :])
                last.then_inc(s["ct_mm"], 1)

            def turn(b):
                pe.wait_ge(s["xe_ev"], b + 1)
                for c in range(4):
                    last = tr(PS[:, 3, 128 * c:128 * c + 128], xe[:, 128 * c:128 * c + 128])
                last.then_inc(s["xt_mm"], 1)

            def combine(b, t):
                if t == 0:
                    pe.wait_ge(s["yy_ready"], b + 2)
                    pe.wait_ge(s["yyl_ready"], b + 2)
                    pe.wait_ge(s["c_ready"], b + 2)
                for h in range(2):
                    pe.wait_ge(s["o_ev"], 6 * (b + 1) + 2 * t + h + 1)
                    for part in range(2):
                        last = mm(PS[0:ROWS[t], 6 + h, :], c01[:, h, TCOL[t]:TCOL[t] + ROWS[t]], yy2[:, part, :],
                                  start=(part == 0), stop=(part == 1))
                    last.then_inc(s["comb_mm"], 1)

            pe.wait_ge(s["route_ready"], 1)
            total = pe.value_load(blocks[0:1, 0:1], min_val=NE, max_val=MAX_BLOCKS)
            gather(0)
            turn(0)
            with pe.Fori(0, total) as b:
                e = pe.value_load(expert_of[0:1, bass.ds(b, 1)], min_val=0, max_val=NE - 1)
                pe.wait_ge(s["xt_ev"], b + 1)
                pe.wait_ge(s["sel_ready"], b + 1)
                pe.wait_ge(s["gu_ev"], b + 1)
                for m in range(2):
                    for part in range(2):
                        mm(bank(m), sel[:, 2 * m:2 * m + 2, :], b_gu2[:, part, :], start=(part == 0), stop=False)
                for c in range(GU_CHUNKS):
                    if c:
                        combine(b - 1, c - 1)
                    pe.wait_ge(w_full[EXPERT_SLOT[c]], expert_arrival(c) + 16 * e)
                    w = ring[:, EXPERT_SLOT[c], :].rearrange("p (k n) -> p k n", k=2)
                    for kk in range(2):
                        k = 2 * c + kk
                        for m in range(2):
                            for h in range(2):
                                last = mm(PS[64 * h:64 * h + 64, m, :], xt[:, k % 4, k // 4, :],
                                          w[:, kk, D * m + 512 * h:D * m + 512 * h + 512],
                                          start=False, stop=(k == KD - 1))
                    last.then_inc(s[("gs_used", "gs_used1", "gs_used2", "gu_mm")[c]], 1)
                gather(b + 1)
                pe.wait_ge(s["act_ready"], 2 * b + 2)
                pe.wait_ge(s["at_ev"], b + 1)
                for c in range(4):
                    last = tr(PS[:, 4, 128 * c:128 * c + 128], ac[:, 128 * c:128 * c + 128])
                last.then_inc(s["at_mm"], 1)
                turn(b + 1)
                pe.wait_ge(s["seld_ready"], b + 1)
                for part in range(2):
                    mm(bank(2), sel_dn[:, :, :], b_dn2[:, part, :], start=(part == 0), stop=False)
                pe.wait_ge(s["at_ev"], b + 2)
                for c in range(DN_CHUNKS):
                    i = GU_CHUNKS + c
                    pe.wait_ge(w_full[EXPERT_SLOT[i]], expert_arrival(i) + 16 * e)
                    w = ring[:, EXPERT_SLOT[i], :].rearrange("p (k n) -> p k n", k=4)
                    for kk in range(4):
                        for h in range(2):
                            last = mm(PS[64 * h:64 * h + 64, 2, :], at[:, kk, c, :],
                                      w[:, kk, 512 * h:512 * h + 512], start=False,
                                      stop=(c == 1 and kk == 3))
                    last.then_inc(s[("ds_used", "d_mm")[c]], 1)
            for t in range(NT):
                combine(total - 1, t)


def head_of(group, n):
    return 4 * group + 2 * (n % 2) + n // 2


def backwards(v, at, n):
    return v[:, :, at:at - n:-1] if at >= n else v[:, :, at::-1]


def mix_bank(i):
    return (7, 1)[i % 3 % 2]


def out_bank(i):
    return 2 + i % 4


def seg_ps(PS, rows):
    v = PS[0:rows, 2:4, 0:4 * rows]
    return v.rearrange("p b (h n) -> p b h n", n=rows)


_INS = ['x_prompt', 'x_sample', 'cache_k', 'cache_v', 'state_conv', 'state_ssm',
        'norm_mix_g', 'w_in', 'conv_w', 'conv_b', 'dt_bias', 'a_log', 'd_skip', 'ssm_norm_g',
        'att_norm_g', 'rel_bias_table', 'w_out', 'norm_ffn_g', 'w_router', 'b_router',
        'w_gate_up', 'b_gate_up', 'w_down', 'b_down', 'norm_final_g']
_OUTS = [(1, SP, D), (1, SS, D), (1, 1, SP, AH, AD), (1, 1, SP, AH, AD), (1, 1, TAPS - 1, D_CONV),
         (1, 1, HEADS, P_HEAD, NSTATE), (1, 1, SS, AH, AD), (1, 1, SS, AH, AD), (1, 1, TAPS - 1, D_CONV),
         (1, 1, HEADS, P_HEAD, NSTATE)]


def kernel(**inputs):
    import numpy as _np
    import concourse.bacc as _bacc
    from concourse import mybir as _mybir
    from concourse.bass_utils import run_bass_kernel_spmd as _run

    nc = _bacc.Bacc("TRN2", target_bir_lowering=False, num_devices=1)
    arrays, args = {}, []
    for name in _INS:
        a = _np.ascontiguousarray(inputs[name])
        arrays[f"in_{name}_dram"] = a
        args.append(nc.dram_tensor(f"in_{name}_dram", a.shape, _mybir.dt.from_np(a.dtype), kind="ExternalInput").ap())
    for i, shape in enumerate(_OUTS):
        args.append(nc.dram_tensor(f"out_{i}_dram", shape, _mybir.dt.float32, kind="ExternalOutput").ap())
    build(nc, *args)
    r = _run(nc, [arrays], core_ids=[0])
    return tuple(r.results[0][f"out_{i}_dram"] for i in range(len(_OUTS)))
```
